# Optimizing a Trainium2 kernel written in Bass

```python
import jax
import jax.numpy as jnp
from jax import lax
import numpy as np

D_MODEL = 1024
BATCH = 1
SEQ = 256
DEPTH = 2

N_HEADS = 8
HEAD_DIM = 64
N_KV = 2
HPG = N_HEADS // N_KV
ROT_DIM = HEAD_DIM // 4
ROPE_THETA = 500000.0
CMP_LEN = 32
CMP_STRIDE = 16
SLC_LEN = 64
SLC_TOPN = 16
WINDOW = 512
Q_BLOCK = 128
SLC_Q_CHUNK = 64
SCALE = HEAD_DIM ** -0.5
NEG = -1e30
FORCE_INIT = 1e6
FORCE_LOCAL = 2e6
POOL_GROUPS = 4
POOL_WINDOWS = (2, 4, 8, 16)
POOL_WIDTH = 512
POOL_GW = POOL_WIDTH // POOL_GROUPS
ATT_WIDTH = N_HEADS * HEAD_DIM
KV_WIDTH = 3 * 2 * N_KV * HEAD_DIM
GATE_NSA = 3 * N_HEADS
MERGE_GATES = 2 * D_MODEL
IN_WIDTH = ATT_WIDTH + KV_WIDTH + GATE_NSA + POOL_WIDTH + MERGE_GATES
SPLITS = (ATT_WIDTH, ATT_WIDTH + KV_WIDTH, ATT_WIDTH + KV_WIDTH + GATE_NSA,
          ATT_WIDTH + KV_WIDTH + GATE_NSA + POOL_WIDTH)
PEER_HEADS = 8
N_KEYS = 128
N_EXPERTS = N_KEYS * N_KEYS
PEER_TOPK = 16
PEER_DK = 128
PEER_CHUNK = 128
DN_ALPHA = (2 * DEPTH) ** 0.25
DN_BETA = (8 * DEPTH) ** -0.25
LN_EPS = 1e-5

kernel_name = 'nsa_pool_peer_hybrid'

def layer_norm(x, g, b):
    xf = x.astype(jnp.float32)
    mu = jnp.mean(xf, -1, keepdims=True)
    var = jnp.mean(jnp.square(xf - mu), -1, keepdims=True)
    return ((xf - mu) * lax.rsqrt(var + LN_EPS) * g + b).astype(x.dtype)

def rope_tables(pos):
    inv = ROPE_THETA ** (-jnp.arange(0, ROT_DIM, 2, dtype=jnp.float32) / ROT_DIM)
    ang = pos.astype(jnp.float32)[:, None] * inv[None, :]
    return jnp.cos(ang), jnp.sin(ang)

def apply_rope(z, cos, sin):
    half = ROT_DIM // 2
    z1, z2, zp = z[..., :half], z[..., half:ROT_DIM], z[..., ROT_DIM:]
    co = cos[:, None, :].astype(z.dtype)
    si = sin[:, None, :].astype(z.dtype)
    return jnp.concatenate([z1 * co - z2 * si, z1 * si + z2 * co, zp], axis=-1)

def compress(z, pe, w1, w2):
    B, S, G, dh = z.shape
    n_cmp = (S - CMP_LEN) // CMP_STRIDE + 1
    idx = jnp.arange(n_cmp)[:, None] * CMP_STRIDE + jnp.arange(CMP_LEN)[None, :]
    blocks = z[:, idx] + pe[:, None, :]
    flat = jnp.moveaxis(blocks, 3, 2).reshape(B, n_cmp, G, CMP_LEN * dh)
    return jax.nn.gelu(flat @ w1) @ w2

def cmp_to_slc(n_cmp, n_slc):
    st = jnp.arange(n_cmp) * CMP_STRIDE
    js = jnp.arange(n_slc) * SLC_LEN
    ov = (jnp.minimum(st[:, None] + CMP_LEN, js[None, :] + SLC_LEN)
          - jnp.maximum(st[:, None], js[None, :]))
    return jnp.maximum(ov, 0).astype(jnp.float32) / CMP_STRIDE

def sel_attend(qg, idx, k, v, t):
    B, S, G, _, dh = qg.shape
    n_slc = S // SLC_LEN
    n_sel = idx.shape[-1]
    kt = k.reshape(B, n_slc, SLC_LEN, G, dh).transpose(0, 3, 1, 2, 4)
    vt = v.reshape(B, n_slc, SLC_LEN, G, dh).transpose(0, 3, 1, 2, 4)
    n_chunk = S // SLC_Q_CHUNK
    bi = jnp.arange(B)[:, None, None, None]
    gi = jnp.arange(G)[None, None, :, None]

    def chunk(args):
        qc, ic, tc = args
        kb = kt[bi, gi, ic]
        vb = vt[bi, gi, ic]
        s = jnp.einsum('bcghd,bcgnld->bcghnl', qc, kb).astype(jnp.float32) * SCALE
        kpos = ic[..., None] * SLC_LEN + jnp.arange(SLC_LEN)
        ok = kpos <= tc[None, :, None, None, None]
        s = jnp.where(ok[:, :, :, None], s, NEG)
        p = jax.nn.softmax(s.reshape(s.shape[:4] + (-1,)), axis=-1).reshape(s.shape)
        return jnp.einsum('bcghnl,bcgnld->bcghd', p.astype(vb.dtype), vb)

    qs = qg.reshape(B, n_chunk, SLC_Q_CHUNK, G, HPG, dh).swapaxes(0, 1)
    isel = idx.reshape(B, n_chunk, SLC_Q_CHUNK, G, n_sel).swapaxes(0, 1)
    ts = t.reshape(n_chunk, SLC_Q_CHUNK)
    o = lax.map(chunk, (qs, isel, ts))
    return o.swapaxes(0, 1).reshape(B, S, G, HPG, dh)

def win_attend(qg, k, v, t):
    B, S, G, _, dh = qg.shape
    nb = S // Q_BLOCK
    nw = WINDOW // Q_BLOCK

    def bands(z):
        zp = jnp.pad(z, ((0, 0), (WINDOW, 0), (0, 0), (0, 0))).reshape(B, nb + nw, Q_BLOCK, G, dh)
        return jnp.concatenate([zp[:, i:i + nb] for i in range(nw + 1)], axis=2)

    kb, vb = bands(k), bands(v)
    qb = qg.reshape(B, nb, Q_BLOCK, G, HPG, dh)
    s = jnp.einsum('bnqghd,bnkgd->bnghqk', qb, kb).astype(jnp.float32) * SCALE
    tq = t.reshape(nb, Q_BLOCK)
    kpos = (jnp.arange(nb) * Q_BLOCK - WINDOW)[:, None] + jnp.arange((nw + 1) * Q_BLOCK)[None, :]
    diff = tq[:, :, None] - kpos[:, None, :]
    ok = (diff >= 0) & (diff < WINDOW) & (kpos[:, None, :] >= 0)
    s = jnp.where(ok[None, :, None, None], s, NEG)
    p = jax.nn.softmax(s, axis=-1)
    o = jnp.einsum('bnghqk,bnkgd->bnqghd', p.astype(vb.dtype), vb)
    return o.reshape(B, S, G, HPG, dh)

def multiscale_pool(p, w_pool, pool_scale):
    B, S, _ = p.shape
    pf = p.reshape(B, S, POOL_GROUPS, POOL_GW).astype(jnp.float32)
    cs = jnp.pad(jnp.cumsum(pf, axis=1), ((0, 0), (1, 0), (0, 0), (0, 0)))
    t = jnp.arange(S)
    win = jnp.array(POOL_WINDOWS)
    lo_idx = jnp.maximum(t[:, None] + 1 - win[None, :], 0)
    lo = cs[:, lo_idx, jnp.arange(POOL_GROUPS)[None, :]]
    cnt = jnp.minimum(t[:, None] + 1, win[None, :]).astype(jnp.float32)
    pooled = (cs[:, 1:] - lo) / cnt[None, :, :, None] - pf
    y = jnp.einsum('bsgc,gcd->bsgd', pooled.astype(p.dtype), w_pool).reshape(B, S, POOL_WIDTH)
    return y * pool_scale

def token_mixer(h, w_in, cmp_pe, cmp_w1, cmp_w2, w_pool, pool_scale, w_lift, w_o, cos, sin, cos_c, sin_c):
    B, S, _ = h.shape
    t = jnp.arange(S)
    q, kv, g_nsa, p_in, g_mrg = jnp.split(h @ w_in, SPLITS, axis=-1)
    q = apply_rope(q.reshape(B, S, N_HEADS, HEAD_DIM), cos, sin).reshape(B, S, N_KV, HPG, HEAD_DIM)
    kv = kv.reshape(B, S, 3, 2, N_KV, HEAD_DIM)

    k_c = apply_rope(compress(kv[:, :, 0, 0], cmp_pe[0], cmp_w1[0], cmp_w2[0]), cos_c, sin_c)
    v_c = compress(kv[:, :, 0, 1], cmp_pe[1], cmp_w1[1], cmp_w2[1])
    n_cmp = k_c.shape[1]
    cmp_end = jnp.arange(n_cmp) * CMP_STRIDE + CMP_LEN - 1
    vis = cmp_end[None, :] <= t[:, None]
    s = jnp.einsum('bsghd,bcgd->bsghc', q, k_c).astype(jnp.float32) * SCALE
    s = jnp.where(vis[None, :, None, None], s, NEG)
    any_vis = jnp.any(vis, axis=-1).astype(jnp.float32)[None, :, None, None, None]
    p_cmp = jax.nn.softmax(s, axis=-1) * any_vis
    o_cmp = jnp.einsum('bsghc,bcgd->bsghd', p_cmp.astype(v_c.dtype), v_c)

    n_slc = S // SLC_LEN
    imp = jnp.einsum('bsghc,cj->bsgj', p_cmp, cmp_to_slc(n_cmp, n_slc))
    blk = jnp.arange(n_slc)
    cur = (t // SLC_LEN)[:, None]
    score = jnp.where((blk[None, :] <= cur)[None, :, None, :], imp, NEG)
    score = jnp.where((blk == 0)[None, None, None, :], FORCE_INIT, score)
    score = jnp.where((blk[None, :] == cur)[None, :, None, :], FORCE_LOCAL, score)
    _, sel_idx = lax.top_k(score, min(SLC_TOPN, n_slc))
    o_slc = sel_attend(q, sel_idx, apply_rope(kv[:, :, 1, 0], cos, sin), kv[:, :, 1, 1], t)

    o_win = win_attend(q, apply_rope(kv[:, :, 2, 0], cos, sin), kv[:, :, 2, 1], t)

    gate = jax.nn.sigmoid(g_nsa.reshape(B, S, N_KV, HPG, 3))
    o_att = (gate[..., 0:1] * o_cmp + gate[..., 1:2] * o_slc
             + gate[..., 2:3] * o_win).reshape(B, S, ATT_WIDTH)

    o_pool = multiscale_pool(p_in, w_pool, pool_scale)

    g_a, g_b = jnp.split(jax.nn.sigmoid(g_mrg), 2, axis=-1)
    merged = g_a * (o_att @ w_lift[0]) + g_b * (o_pool @ w_lift[1])
    return merged @ w_o

def peer_ffn(h, w_pq, sub_keys, u_tab, v_tab):
    B, S, D = h.shape
    q = (h @ w_pq).reshape(B, S, PEER_HEADS, 2, PEER_DK // 2)
    s = jnp.einsum('bshpd,hpkd->bshpk', q, sub_keys).astype(jnp.float32)
    s1, i1 = lax.top_k(s[..., 0, :], PEER_TOPK)
    s2, i2 = lax.top_k(s[..., 1, :], PEER_TOPK)
    cand = (s1[..., :, None] + s2[..., None, :]).reshape(B, S, PEER_HEADS, -1)
    cand_idx = (i1[..., :, None] * N_KEYS + i2[..., None, :]).reshape(B, S, PEER_HEADS, -1)
    sv, si = lax.top_k(cand, PEER_TOPK)
    eidx = jnp.take_along_axis(cand_idx, si, axis=-1)
    g = jax.nn.softmax(sv, axis=-1)
    n_chunk = (B * S) // PEER_CHUNK
    hf = h.reshape(n_chunk, PEER_CHUNK, D)
    ef = eidx.reshape(n_chunk, PEER_CHUNK, PEER_HEADS * PEER_TOPK)
    gf = g.reshape(n_chunk, PEER_CHUNK, PEER_HEADS * PEER_TOPK).astype(h.dtype)

    def body(args):
        hc, ec, gc = args
        a = jax.nn.gelu(jnp.einsum('cd,ced->ce', hc, u_tab[ec]))
        return jnp.einsum('ce,ced->cd', gc * a, v_tab[ec])

    return lax.map(body, (hf, ef, gf)).reshape(B, S, D)

def setup_inputs(seed: int = 0) -> dict:
    key = jax.random.key(seed)
    ks = jax.random.split(key, 20)
    f32 = jnp.float32
    nrm = lambda k, shp, sc: jax.random.normal(k, shp, f32) * sc
    return {
        'x': nrm(ks[0], (BATCH, SEQ, D_MODEL), 1.0),
        'c': nrm(ks[1], (BATCH, D_MODEL), 1.0),
        'w_ada': nrm(ks[2], (DEPTH, D_MODEL, 6 * D_MODEL), D_MODEL ** -0.5),
        'b_ada': nrm(ks[3], (DEPTH, 6 * D_MODEL), 0.02),
        'w_in': nrm(ks[4], (DEPTH, D_MODEL, IN_WIDTH), D_MODEL ** -0.5),
        'cmp_pe': nrm(ks[5], (DEPTH, 2, CMP_LEN, HEAD_DIM), 0.02),
        'cmp_w1': nrm(ks[6], (DEPTH, 2, CMP_LEN * HEAD_DIM, HEAD_DIM), (CMP_LEN * HEAD_DIM) ** -0.5),
        'cmp_w2': nrm(ks[7], (DEPTH, 2, HEAD_DIM, HEAD_DIM), HEAD_DIM ** -0.5),
        'w_pool': nrm(ks[8], (DEPTH, POOL_GROUPS, POOL_GW, POOL_GW), POOL_GW ** -0.5),
        'pool_scale': 1.0 + nrm(ks[9], (DEPTH, POOL_WIDTH), 0.02),
        'w_lift': nrm(ks[10], (DEPTH, 2, ATT_WIDTH, D_MODEL), ATT_WIDTH ** -0.5),
        'w_o': nrm(ks[11], (DEPTH, D_MODEL, D_MODEL), D_MODEL ** -0.5 * DN_BETA),
        'ln_g': 1.0 + nrm(ks[12], (DEPTH, 2, D_MODEL), 0.02),
        'ln_b': nrm(ks[13], (DEPTH, 2, D_MODEL), 0.02),
        'peer_wq': nrm(ks[14], (DEPTH, D_MODEL, PEER_HEADS * PEER_DK), D_MODEL ** -0.5),
        'peer_keys': nrm(ks[15], (DEPTH, PEER_HEADS, 2, N_KEYS, PEER_DK // 2), (PEER_DK // 2) ** -0.5),
        'peer_u': nrm(ks[16], (DEPTH, N_EXPERTS, D_MODEL), D_MODEL ** -0.5),
        'peer_v': nrm(ks[17], (DEPTH, N_EXPERTS, D_MODEL), (PEER_HEADS * PEER_TOPK) ** -0.5 * DN_BETA),
    }

def reference(x, c, w_ada, b_ada, w_in, cmp_pe, cmp_w1, cmp_w2, w_pool, pool_scale, w_lift, w_o,
              ln_g, ln_b, peer_wq, peer_keys, peer_u, peer_v):
    S = x.shape[1]
    cos, sin = rope_tables(jnp.arange(S))
    n_cmp = (S - CMP_LEN) // CMP_STRIDE + 1
    cos_c, sin_c = rope_tables(jnp.arange(n_cmp) * CMP_STRIDE + CMP_LEN - 1)
    c_act = jax.nn.silu(c)
    for l in range(DEPTH):
        mods = c_act @ w_ada[l] + b_ada[l]
        sh1, sc1, g1, sh2, sc2, g2 = [m[:, None, :] for m in jnp.split(mods, 6, axis=-1)]
        h = x * (1.0 + sc1) + sh1
        y = token_mixer(h, w_in[l], cmp_pe[l], cmp_w1[l], cmp_w2[l], w_pool[l], pool_scale[l],
                        w_lift[l], w_o[l], cos, sin, cos_c, sin_c)
        x = layer_norm(DN_ALPHA * x + g1 * y, ln_g[l, 0], ln_b[l, 0])
        h = x * (1.0 + sc2) + sh2
        y = peer_ffn(h, peer_wq[l], peer_keys[l], peer_u[l], peer_v[l])
        x = layer_norm(DN_ALPHA * x + g2 * y, ln_g[l, 1], ln_b[l, 1])
    return x


_drawn_inputs = setup_inputs


def setup_inputs(seed=0):
    import zlib

    import numpy as np

    out = dict(_drawn_inputs(seed))
    spreads = {}
    factors = {'b_ada': 6.347,
     'cmp_pe': 26.477,
     'pool_scale': 8.0,
     'peer_wq': 3.019,
     'peer_keys': 3.016,
     'peer_u': 3.426,
     'peer_v': 3.04}
    for name, (base, spread) in spreads.items():
        noise = np.random.default_rng([zlib.crc32(name.encode()), seed]).standard_normal(out[name].shape)
        drawn = base * np.exp(spread * noise) if base else spread * noise
        out[name] = jnp.asarray(drawn.astype(out[name].dtype))
    for name, factor in factors.items():
        out[name] = (out[name] * factor).astype(out[name].dtype)
    return out
```

```python
import concourse.bass as bass
from concourse import mybir
import numpy as np

F32 = mybir.dt.float32
F32R = mybir.dt.float32r
BF16 = mybir.dt.bfloat16
U32 = mybir.dt.uint32
ACT = mybir.ActivationFunctionType
ALU = mybir.AluOpType
AX = mybir.AxisListType.X

P = 128
D = 1024
T = 256
L = 2
KT = D // P
TT = T // P
HEADS, HD, GROUPS = 8, 64, 2
HPG = HEADS // GROUPS
CMP_LEN, CMP_STRIDE = 32, 16
N_CMP = (T - CMP_LEN) // CMP_STRIDE + 1
CP = 16
ROT = HD // 4
POOL_G = 4
POOL_W = (2, 4, 8, 16)
PAD = 16
PH, NK, TOPK = 8, 128, 16
SCALE = HD ** -0.5
NEG = -1e30
ALPHA = float((2 * L) ** 0.25)
EPS = 1e-5

RING = 4
ADA = 6 * KT
N_ADA = L * ADA
S_PROJ = 31
S_LIFT = S_PROJ
S_OUT = S_LIFT + KT
S_QUERY = S_OUT + KT
S_KEYS = S_QUERY + PH
S_UP = S_KEYS + 1
S_DOWN = S_UP + NK
SLOTS = S_DOWN + NK
AHEAD = 3

K_IDENT, K_PERM, K_IOTA, K_ONES, KEEP = 0, P, 2 * P, 3 * P, 4 * P
M_ROPE = 0
M_CROPE = M_ROPE + 4 * T
M_CMASK = M_CROPE + 2 * CP
M_ANY = M_CMASK + TT * CP
M_VSEL = M_ANY + TT
M_CNT = M_VSEL + HPG * P
MIX = M_CNT + POOL_G * T
W_CMP1 = 0
W_CMP2 = W_CMP1 + 2 * CMP_LEN * P
W_PE = W_CMP2 + 2 * P
W_POOL = W_PE + 2 * CMP_LEN
W_PSC = W_POOL + POOL_G * P
PACK = W_PSC + POOL_G


class Signal:

    def __init__(self, nc, name, per_layer, before=0):
        self.sem = nc.alloc_semaphore(name)
        self.per_layer, self.before = per_layer, before

    def at(self, layer, n):
        return layer * self.per_layer + (n + self.before)


def program(nc, stream, x_in, c_in, b_ada, pack, ln_gb, const_keep, const_mix, const_bf, out):
    base = (nc.sbuf_base + 63) // 64 * 64
    top = [base]

    def keep(name, shape, dtype=F32, size=4):
        t = nc.alloc_sbuf_tensor_at(name, [P] + shape, dtype, offset=top[0])
        top[0] += (int(np.prod(shape)) * size + 31) // 32 * 32
        return t

    raw = keep("raw", [RING, D])
    w_hi = keep("w_hi", [RING, D], F32R)
    w_lo = keep("w_lo", [RING, D], F32R)
    act_at = top[0]
    act1_hi = keep("act1_hi", [KT, T], F32R)
    act1_lo = keep("act1_lo", [KT, T], F32R)
    x_sb = keep("x_sb", [TT, D])
    sel = keep("sel", [3, T])
    kc = keep("kc", [KEEP])
    bfc = keep("bfc", [2 * P], BF16, 2)
    mods = keep("mods", [N_ADA])
    mods_l = keep("mods_l", [ADA])
    acc4 = keep("acc4", [RING])
    stat = keep("stat", [TT, 2, 6])
    mv = keep("mv", [TT, 2])
    v_eps = keep("v_eps", [TT])
    std = keep("std", [TT])
    rinv = keep("rinv", [TT])
    newt = keep("newt", [TT])
    nbias = keep("nbias", [TT])
    oh2 = nc.alloc_sbuf_tensor_at("oh2", [P, 4, 4, P], F32, offset=act_at)
    oh1g = nc.alloc_sbuf_tensor_at("oh1g", [P, 2, 4, P], F32, offset=act_at + 8192)
    g_hi = nc.alloc_sbuf_tensor_at("g_hi", [P, 2, 4, T], F32R, offset=act_at)
    g_lo = nc.alloc_sbuf_tensor_at("g_lo", [P, 2, 4, T], F32R, offset=act_at + 8192)

    big_at = (top[0] + 63) // 64 * 64
    experts = nc.alloc_sbuf_tensor_at("experts", [P, NK, T], F32, offset=big_at)
    off = [0]

    def mix(name, shape, dtype=F32, at=None):
        n = int(np.prod(shape))
        a = off[0] if at is None else at
        if at is None:
            off[0] += (n + 7) // 8 * 8
        assert a + n <= NK * T, (name, a + n)
        return nc.alloc_sbuf_tensor_at(name, [P] + shape, dtype, offset=big_at + 4 * a), a

    act0_hi, _ = mix("act0_hi", [KT, T], F32R)
    act0_lo, _ = mix("act0_lo", [KT, T], F32R)
    hf, hf_at = mix("hf", [KT, T])
    z_ln, _ = mix("z_ln", [TT, D], at=hf_at)
    opf, _ = mix("opf", [POOL_G, T], at=hf_at)
    mf, _ = mix("mf", [2, T], at=hf_at + POOL_G * T)
    wp, wp_at = mix("wp", [PACK])
    cm, _ = mix("cm", [MIX])
    qk_raw, qk_raw_at = mix("qk_raw", [8, T])
    prod, _ = mix("prod", [2, 2, T], at=qk_raw_at)
    qk, _ = mix("qk", [6, T])
    zpe, zpe_at = mix("zpe", [2, 2, T])
    prob_t, _ = mix("prob_t", [2, 2 * T], at=zpe_at)
    vtok, _ = mix("vtok", [2, T])
    gate3, _ = mix("gate3", [TT, 24])
    pin, _ = mix("pin", [POOL_G, PAD + T])
    psum2, _ = mix("psum2", [2, PAD + T])
    pooled, _ = mix("pooled", [POOL_G, T])
    gab, _ = mix("gab", [KT, 2, T])
    hid_k, _ = mix("hid_k", [CP])
    hid_v, _ = mix("hid_v", [HEADS, CP])
    kc_raw, _ = mix("kc_raw", [CP])
    kc_t1, _ = mix("kc_t1", [CP])
    kc_rot, _ = mix("kc_rot", [CP])
    vc_sel, _ = mix("vc_sel", [HPG, P])
    pc, _ = mix("pc", [TT, HEADS, CP])
    pc_m, _ = mix("pc_m", [TT, HEADS])
    pc_t, _ = mix("pc_t", [TT, P])
    prob, _ = mix("prob", [2, 2 * T])
    nmax, _ = mix("nmax", [2 * HEADS, 2])
    rsum, _ = mix("rsum", [2 * HEADS, 2])
    rope_t, _ = mix("rope_t", [2, T])
    ln_row, _ = mix("ln_row", [2, D], at=wp_at)
    g_row, _ = mix("g_row", [D], at=wp_at + 2 * D)
    diag, _ = mix("diag", [KT, P], at=wp_at + 3 * D)
    q_hi, _ = mix("q_hi", [PH, T], F32R, at=64 * T)
    q_lo, _ = mix("q_lo", [PH, T], F32R, at=72 * T)
    r_at = 96 * T
    scores, _ = mix("scores", [2 * PH, 2, NK], at=r_at)
    r_at += 2 * PH * 2 * NK
    sv, _ = mix("sv", [2 * PH, TOPK], at=r_at)
    ci, _ = mix("ci", [2 * PH, TOPK], U32, at=r_at + 256)
    ij, _ = mix("ij", [2 * PH, 2, TOPK], U32, at=r_at + 512)
    half_v, _ = mix("half_v", [2, TOPK], at=r_at + 1024)
    work, _ = mix("work", [2, NK], at=r_at + 1056)
    cand, _ = mix("cand", [TOPK, TOPK], at=r_at + 1312)
    cand2, _ = mix("cand2", [TOPK, TOPK], at=r_at + 1568)
    ab, _ = mix("ab", [2, TOPK], U32, at=r_at + 1824)
    onehot, _ = mix("onehot", [2, TOPK, TOPK], at=r_at + 1856)
    rsm, _ = mix("rsm", [2 * PH], at=r_at + 2368)
    work_s, _ = mix("work_s", [2, NK], at=r_at + 2384)
    sv_s, _ = mix("sv_s", [TOPK], at=r_at + 2640)
    ci_s, _ = mix("ci_s", [TOPK], U32, at=r_at + 2656)
    ij_s, _ = mix("ij_s", [2, TOPK], U32, at=r_at + 2672)
    ij_f, _ = mix("ij_f", [2, TOPK], at=r_at + 2704)
    c_silu, _ = mix("c_silu", [D], at=0)
    bf_stage, _ = mix("bf_stage", [2 * P], at=D)
    assert top[0] <= big_at and big_at + 4 * NK * T <= nc.sbuf_usable_end, (big_at, nc.sbuf_usable_end)

    ps = nc.alloc_psum_tensor("ps", [P, 8, 512], F32)
    ident, perm = kc[:, K_IDENT:K_IDENT + P], kc[:, K_PERM:K_PERM + P]
    iota, ones = kc[:, K_IOTA:K_IOTA + P], kc[:, K_ONES:K_ONES + P]
    ident_bf, mask_bf = bfc[:, 0:P], bfc[:, P:2 * P]
    rope = cm[:, M_ROPE:M_ROPE + 4 * T].rearrange("p (a t) -> p a t", a=4)
    crope = cm[:, M_CROPE:M_CROPE + 2 * CP].rearrange("p (a c) -> p a c", a=2)
    cmask = cm[:, M_CMASK:M_CMASK + TT * CP].rearrange("p (a c) -> p a c", a=TT)
    any_vis = cm[:, M_ANY:M_ANY + TT]
    vsel = cm[:, M_VSEL:M_VSEL + HPG * P].rearrange("p (a c) -> p a c", a=HPG)
    inv_cnt = cm[:, M_CNT:M_CNT + POOL_G * T].rearrange("p (a c) -> p a c", a=POOL_G)
    cmp_w1 = wp[:, W_CMP1:W_CMP2].rearrange("p (a l m) -> p a l m", a=2, l=CMP_LEN)
    cmp_w2 = wp[:, W_CMP2:W_PE].rearrange("p (a m) -> p a m", a=2)
    cmp_pe = wp[:, W_PE:W_POOL].rearrange("p (a l) -> p a l", a=2)
    w_pool = wp[:, W_POOL:W_PSC].rearrange("p (a m) -> p a m", a=POOL_G)
    pool_sc = wp[:, W_PSC:PACK]

    def sig(name, per_layer, before=0):
        return Signal(nc, name, per_layer, before)

    raw_loaded = [sig(f"raw_loaded{r}", 16 * SLOTS // RING, 16 * N_ADA // RING) for r in range(RING)]
    raw_done = sig("raw_done", SLOTS, N_ADA + RING)
    hi_ready = sig("hi_ready", SLOTS)
    slot_used = sig("slot_used", SLOTS, RING)
    start_loaded = sig("start_loaded", 0)
    c_exp = sig("c_exp", 0)
    x_ready = sig("x_ready", 2, 1)
    params_loaded = sig("params_loaded", 32)
    ln_loaded = sig("ln_loaded", 64)
    mods_ready = sig("mods_ready", 1)
    xt_done = sig("xt_done", 8)
    hf_done = sig("hf_done", 8)
    h_ready = sig("h_ready", 4)
    proj_out = sig("proj_out", S_PROJ)
    perm_done = sig("perm_done", 7)
    rope_done = sig("rope_done", 7)
    zpe_done = sig("zpe_done", 2)
    pads_zero = sig("pads_zero", 1)
    hid_zero = sig("hid_zero", 1)
    cmp_hid = sig("cmp_hid", 1)
    cmp_gelu = sig("cmp_gelu", 1)
    cmp_kv = sig("cmp_kv", 1)
    cmp_kraw = sig("cmp_kraw", 1)
    cmp_vsel = sig("cmp_vsel", 1)
    cmp_scored = sig("cmp_scored", 1)
    cmp_shift = sig("cmp_shift", 1)
    cmp_exp = sig("cmp_exp", 1)
    cmp_prob = sig("cmp_prob", 1)
    cmp_turned = sig("cmp_turned", 1)
    cmp_pt = sig("cmp_pt", 1)
    scored = sig("scored", 16)
    maxed = sig("maxed", 16)
    exped = sig("exped", 16)
    prob_ready = sig("prob_ready", 16)
    turned = sig("turned", 16)
    pt_out = sig("pt_out", 16)
    pv_done = sig("pv_done", 16)
    o_hi = sig("o_hi", 2)
    o_ready = sig("o_ready", 2)
    pooled_ready = sig("pooled_ready", POOL_G)
    pool_mixed = sig("pool_mixed", 2)
    pool_hi = sig("pool_hi", 2)
    pool_ready = sig("pool_ready", 2)
    lift_read = sig("lift_read", KT)
    merged = sig("merged", KT)
    merged_hi = sig("merged_hi", KT)
    merged_ready = sig("merged_ready", KT)
    diag_ready = sig("diag_ready", 2)
    gate_spread = sig("gate_spread", 2)
    gate_row = sig("gate_row", 2)
    var_ready = sig("var_ready", 2)
    std_ready = sig("std_ready", 2)
    shift_ready = sig("shift_ready", 2)
    normed = sig("normed", 4)
    q_hi_out = sig("q_hi_out", PH)
    q_ready = sig("q_ready", PH)
    keys_scored = sig("keys_scored", PH - 1)
    scores_out = sig("scores_out", PH)
    gelu_done = sig("gelu_done", NK)
    sel_shift = sig("sel_shift", 1)
    sel_exp = sig("sel_exp", 1)
    routed = sig("routed", 1)
    sel_turned = sig("sel_turned", 1)
    sel_out = sig("sel_out", 1)
    oh2_diff = sig("oh2_diff", T // 4)
    oh2_ready = sig("oh2_ready", T // 4)
    oh1_ready = sig("oh1_ready", T // 4)
    gates_done = sig("gates_done", T // 4)
    gates_applied = sig("gates_applied", T // 4)
    g_hi_out = sig("g_hi_out", NK // 4)
    g_ready = sig("g_ready", NK // 4)
    stored = sig("stored", 0)

    def mod(j):
        return mods_l[:, j * KT:(j + 1) * KT]

    with nc.Block() as block:

        @block.sync
        def _(sp):
            sp.dma_start(raw[:, 0, :], c_in.to_broadcast([P, D])).then_inc(start_loaded.sem, 16)
            sp.dma_start(kc[:], const_keep).then_inc(start_loaded.sem, 16)
            sp.dma_start(bf_stage[:], const_bf).then_inc(start_loaded.sem, 16)
            sp.dma_start(mods[:], b_ada).then_inc(start_loaded.sem, 16)
            sp.dma_start(x_sb[:], x_in.rearrange("o (a p) d -> p (o a) d", p=P)).then_inc(start_loaded.sem, 16)
            with sp.Fori(0, (N_ADA + L * SLOTS) // RING) as j:
                for r in range(RING):
                    sp.wait_ge(raw_done.sem, RING * j + r + 1)
                    sp.dma_start(raw[:, r, :], stream[RING * j + r]).then_inc(raw_loaded[r].sem, 16)
            sp.wait_ge(x_ready.sem, x_ready.at(L - 1, 2))
            sp.dma_start(out.rearrange("o (a p) d -> p (o a) d", p=P), x_sb[:]).then_inc(stored.sem, 16)
            sp.wait_ge(stored.sem, 16)

        @block.gpsimd
        def _(pool):
            with pool.Fori(0, L) as l:
                pool.wait_ge(x_ready.sem, x_ready.at(l, 0))
                pool.nop()
                pool.dma_start(wp[:], pack[l]).then_inc(params_loaded.sem, 16)
                pool.dma_start(cm[:], const_mix).then_inc(params_loaded.sem, 16)
                pool.memset(pin[:, :, 0:PAD], 0.0)
                pool.memset(psum2[:, :, 0:PAD], 0.0).then_inc(pads_zero.sem, 1)
                pool.wait_ge(params_loaded.sem, params_loaded.at(l, 32))
                for g in range(POOL_G):
                    pool.wait_ge(proj_out.sem, proj_out.at(l, 12 + g))
                    cur = pin[:, g, :]
                    for k in range(g + 1):
                        nxt, s = psum2[:, k % 2, :], 1 << k
                        if k:
                            pool.drain()
                        pool.tensor_tensor(nxt[:, PAD:], cur[:, PAD:], cur[:, PAD - s:PAD + T - s], ALU.add)
                        cur = nxt
                    pool.drain()
                    pool.tensor_tensor(pooled[:, g, :], cur[:, PAD:], inv_cnt[:, g, :], ALU.mult)
                    pool.drain()
                    pool.tensor_tensor(pooled[:, g, :], pooled[:, g, :], pin[:, g, PAD:], ALU.subtract).then_inc(pooled_ready.sem, 1)
                pool.wait_ge(cmp_hid.sem, cmp_hid.at(l, 1))
                pool.nop()
                pool.dma_start(ln_row[:, 0, :], ln_gb[l, 0].to_broadcast([P, D])).then_inc(ln_loaded.sem, 16)
                pool.dma_start(ln_row[:, 1, :], ln_gb[l, 1].to_broadcast([P, D])).then_inc(ln_loaded.sem, 16)
                pool.wait_ge(ln_loaded.sem, ln_loaded.at(l, 32))
                pool.wait_ge(sel_out.sem, sel_out.at(l, 1))
                pool.nop()

                def distance(k, b):
                    pool.tensor_tensor(oh2[:, b], iota.unsqueeze(1).to_broadcast([P, 4, P]),
                                       sel[:, 1, bass.ds(4 * k, 4)].unsqueeze(2).to_broadcast([P, 4, P]),
                                       ALU.subtract).then_inc(oh2_diff.sem, 1)

                for b in range(4):
                    distance(b, b)
                with pool.Fori(1, T // 16) as i:
                    for b in range(4):
                        pool.wait_ge(gates_done.sem, gates_done.at(l, 4 * i + (b - 3)))
                        pool.nop()
                        distance(4 * i + b, b)
                pool.wait_ge(g_ready.sem, g_ready.at(l, NK // 4))
                pool.nop()
                pool.dma_start(ln_row[:, 0, :], ln_gb[l, 2].to_broadcast([P, D])).then_inc(ln_loaded.sem, 16)
                pool.dma_start(ln_row[:, 1, :], ln_gb[l, 3].to_broadcast([P, D])).then_inc(ln_loaded.sem, 16)

        @block.scalar
        def _(act):
            def hi(l, j, i):
                r = i % RING
                act.wait_ge(raw_loaded[r].sem, raw_loaded[r].at(l, 16 * (j + i // RING + 1)))
                act.wait_ge(slot_used.sem, l * SLOTS + RING * j + (i + 1))
                act.activation(w_hi[:, r, :], raw[:, r, :], ACT.Copy).then_inc(hi_ready.sem, 1)

            def product(l, j, i):
                act.wait_ge(slot_used.sem, slot_used.at(l, RING * j + (i + 1)))

            def build_h(l, which, banks):
                sc, sh = mod(3 * which + 1), mod(3 * which)
                act.wait_ge(mods_ready.sem, mods_ready.at(l, 1))
                for k in range(KT):
                    if k % 2 == 0:
                        act.wait_ge(xt_done.sem, xt_done.at(l, 4 * which + k // 2 + 1))
                    a = act.activation(hf[:, k, :], ps[:, banks + k // 2, (k % 2) * T:(k % 2 + 1) * T], ACT.Identity,
                                       scale=sc[:, k:k + 1], bias=sh[:, k:k + 1])
                    if k % 2:
                        a.then_inc(hf_done.sem, 1)

            def norm(l, which, gate_bank):
                act.wait_ge(gate_spread.sem, gate_spread.at(l, which + 1))
                act.copy(g_row[:, 0:512], ps[:, gate_bank, :])
                act.copy(g_row[:, 512:1024], ps[:, gate_bank + 1, :]).then_inc(gate_row.sem, 1)

            def norm_end(l, which):
                act.wait_ge(var_ready.sem, var_ready.at(l, which + 1))
                act.activation(std[:], v_eps[:], ACT.Sqrt).then_inc(std_ready.sem, 1)
                act.wait_ge(shift_ready.sem, shift_ready.at(l, which + 1))
                for t in range(TT):
                    act.activation(x_sb[:, t, :], z_ln[:, t, :], ACT.Identity, scale=rinv[:, t:t + 1],
                                   bias=nbias[:, t:t + 1]).then_inc(normed.sem, 1)

            def attend(l, n):
                if n < 16:
                    w = (n // HEADS + 1) * P
                    act.wait_ge(maxed.sem, maxed.at(l, n + 1))
                    if n >= 2:
                        act.wait_ge(turned.sem, turned.at(l, n - 1))
                    for b in range(2):
                        a = act.activation(prob[:, n % 2, b * w:(b + 1) * w], ps[:, 2 + n % 2, b * w:(b + 1) * w], ACT.Exp,
                                           bias=nmax[:, n, b:b + 1], scale=1.0, accum_out=rsum[:, n, b:b + 1])
                    a.then_inc(exped.sem, 1)
                if 1 <= n <= 16:
                    u = n - 1
                    w = 2 * (u // HEADS + 1) * P
                    act.wait_ge(turned.sem, turned.at(l, u + 1))
                    if u >= 2:
                        act.wait_ge(pv_done.sem, pv_done.at(l, u - 1))
                    act.copy(prob_t[:, u % 2, 0:w], ps[:, 4 + u % 2, 0:w]).then_inc(pt_out.sem, 1)
                if n in (10, 17):
                    t = n // 16
                    act.wait_ge(pv_done.sem, pv_done.at(l, HEADS * (t + 1)))
                    act.activation(act1_hi[:, 0:HPG, t * P:(t + 1) * P], ps[:, 6 + t, :].rearrange("p (c t) -> p c t", c=HPG),
                                   ACT.Copy).then_inc(o_hi.sem, 1)

            act.wait_ge(start_loaded.sem, 80)
            act.activation(c_silu[:], raw[:, 0, :], ACT.Exp, scale=-1.0).then_inc(c_exp.sem, 1)

            with act.Fori(0, L) as l:
                for i in range(AHEAD):
                    hi(l, 0, i)
                build_h(l, 0, 2)
                for s in range(S_PROJ):
                    hi(l, 0, s + AHEAD)
                    product(l, 0, s)
                    bank = ps[:, s % 2, 0:T]
                    if s < 8:
                        a = act.copy(qk_raw[:, s, :], bank)
                    elif s < 10:
                        a = act.copy(vtok[:, s - 8, :], bank)
                    elif s == 10:
                        a = act.activation(gate3[:], bank.rearrange("p (a c) -> p a c", a=TT)[:, :, 0:24], ACT.Tanh, scale=0.5)
                    elif s < 15:
                        if s == 11:
                            act.wait_ge(pads_zero.sem, pads_zero.at(l, 1))
                        a = act.copy(pin[:, s - 11, PAD:], bank)
                    else:
                        a = act.activation(gab[:, (s - 15) % KT, (s - 15) // KT, :], bank, ACT.Tanh, scale=0.5)
                    a.then_inc(proj_out.sem, 1)
                    if s == 9:
                        act.wait_ge(cmp_hid.sem, cmp_hid.at(l, 1))
                        act.wait_ge(hid_zero.sem, hid_zero.at(l, 1))
                        act.activation(hid_k[:, 0:N_CMP], ps[:, 6, 0:N_CMP], ACT.Gelu_apprx_tanh)
                        act.activation(hid_v[:, :, 0:N_CMP], ps[:, 6, CP:CP + N_CMP].unsqueeze(1).to_broadcast([P, HEADS, N_CMP]),
                                       ACT.Gelu_apprx_tanh).then_inc(cmp_gelu.sem, 1)
                    if s == 14:
                        act.wait_ge(cmp_shift.sem, cmp_shift.at(l, 1))
                        act.activation(pc[:], pc[:], ACT.Exp).then_inc(cmp_exp.sem, 1)
                    if s == 15:
                        act.wait_ge(cmp_turned.sem, cmp_turned.at(l, 1))
                        act.copy(pc_t[:], ps[:, 7, 0:TT * P].rearrange("p (a c) -> p a c", a=TT)).then_inc(cmp_pt.sem, 1)
                    if s >= 15:
                        attend(l, s - 15)
                for u in (16, 17):
                    attend(l, u)
                for n in range(2):
                    act.wait_ge(pool_mixed.sem, pool_mixed.at(l, n + 1))
                    for g in (2 * n, 2 * n + 1):
                        act.activation(opf[:, g, :], ps[:, 2 + n, (g % 2) * T:(g % 2 + 1) * T], ACT.Copy, scale=pool_sc[:, g:g + 1])
                    act.drain()
                    act.activation(act1_hi[:, 4 + 2 * n:6 + 2 * n, :], opf[:, 2 * n:2 * n + 2, :], ACT.Copy).then_inc(pool_hi.sem, 1)
                for k in range(KT):
                    s = S_LIFT + k
                    hi(l, 0, s + AHEAD)
                    act.wait_ge(merged.sem, merged.at(l, k + 1))
                    act.activation(act0_hi[:, k, :], mf[:, k % 2, :], ACT.Copy).then_inc(merged_hi.sem, 1)
                norm(l, 0, 6)
                for k in range(KT):
                    hi(l, 0, S_OUT + k + AHEAD)
                norm_end(l, 0)
                build_h(l, 1, 2)
                for k in range(PH):
                    hi(l, 0, S_QUERY + k + AHEAD)
                    product(l, 0, S_QUERY + k)
                    act.activation(q_hi[:, k, :], ps[:, (S_QUERY + k) % 2, 0:T], ACT.Copy).then_inc(q_hi_out.sem, 1)
                hi(l, 0, S_KEYS + AHEAD)
                for k in range(PH):
                    if k < PH - 1:
                        act.wait_ge(keys_scored.sem, keys_scored.at(l, k + 1))
                    else:
                        product(l, 0, S_KEYS)
                    act.copy(scores[:, 2 * k:2 * k + 2].rearrange("p u h k -> p h u k"),
                             ps[:, 2 + 2 * (k % 2):4 + 2 * (k % 2), 0:2 * NK].rearrange("p h (u k) -> p h u k", u=2)).then_inc(scores_out.sem, 1)

                def up(i):
                    for n in range(RING):
                        hi(l, i + S_UP // RING, n + AHEAD)
                        product(l, i + S_UP // RING, n)
                        act.nop()
                        act.activation(experts[:, RING * i + n, :], ps[:, n % 2, 0:T], ACT.Gelu_apprx_tanh).then_inc(gelu_done.sem, 1)

                with act.Fori(0, 16) as i:
                    up(i)
                with act.Fori(16, 24) as i:
                    up(i)
                act.wait_ge(sel_shift.sem, sel_shift.at(l, 1))
                act.activation(sv[:], sv[:], ACT.Exp).then_inc(sel_exp.sem, 1)
                act.wait_ge(routed.sem, routed.at(l, 1))
                with act.Fori(24, 32) as i:
                    up(i)
                act.wait_ge(sel_turned.sem, sel_turned.at(l, 1))
                act.copy(sel[:, 0:2, :].rearrange("p a t -> p (a t)"), ps[:, 2, :])
                act.copy(sel[:, 2, :], ps[:, 3, 0:T]).then_inc(sel_out.sem, 1)

                def one_hot(k, b):
                    act.wait_ge(oh2_diff.sem, oh2_diff.at(l, k + 1))
                    act.activation(oh2[:, b], oh2[:, b], ACT.Abs)
                    act.drain()
                    act.activation(oh2[:, b], oh2[:, b], ACT.Relu, scale=-1.0, bias=1.0).then_inc(oh2_ready.sem, 1)

                with act.Fori(0, T // 16) as i:
                    for b in range(4):
                        one_hot(4 * i + b, b)
                act.wait_ge(gates_applied.sem, gates_applied.at(l, T // 4))

                def gated(i, b):
                    act.activation(g_hi[:, b].rearrange("p a t -> p (a t)"),
                                   experts[:, bass.ds(RING * i, RING), :].rearrange("p a t -> p (a t)"), ACT.Copy).then_inc(g_hi_out.sem, 1)

                def down(i, b, more=True):
                    hi(l, i + S_DOWN // RING, AHEAD)
                    if more:
                        gated(i + 1, b)
                        for n in range(1, RING):
                            hi(l, i + S_DOWN // RING, n + AHEAD)

                gated(0, 0)
                down(0, 1)
                with act.Fori(0, 15) as h:
                    down(2 * h + 1, 0)
                    down(2 * h + 2, 1)
                down(NK // 4 - 1, None, more=False)
                norm(l, 1, 2)
                norm_end(l, 1)

        @block.vector
        def _(dve):
            def lo(l, j, i):
                r = i % RING
                dve.wait_ge(hi_ready.sem, hi_ready.at(l, RING * j + (i + 1)))
                dve.tensor_tensor(w_lo[:, r, :], raw[:, r, :], w_hi[:, r, :].bitcast(F32), ALU.subtract).then_inc(raw_done.sem, 1)

            def build_h(l, which, dst_hi, dst_lo):
                for n in range(2):
                    dve.wait_ge(hf_done.sem, hf_done.at(l, 4 * which + 2 * n + 2))
                    a, b = KT // 2 * n, KT // 2 * (n + 1)
                    dve.tensor_copy(dst_hi[:, a:b, :], hf[:, a:b, :])
                    dve.drain()
                    dve.tensor_tensor(dst_lo[:, a:b, :], hf[:, a:b, :], dst_hi[:, a:b, :].bitcast(F32), ALU.subtract).then_inc(h_ready.sem, 1)

            def gate_diag(l, which):
                g = mod(3 * which + 2)
                for k in range(KT):
                    d = dve.tensor_scalar(diag[:, k, :], ident, g[:, k:k + 1], None, ALU.mult)
                d.then_inc(diag_ready.sem, 1)

            def norm(l, which, bank, last_slot):
                dve.wait_ge(gate_row.sem, gate_row.at(l, which + 1))
                dve.wait_ge(slot_used.sem, slot_used.at(l, last_slot + 1))
                for t in range(TT):
                    for h in range(2):
                        c = slice(512 * h, 512 * h + 512)
                        dve.tensor_tensor(z_ln[:, t, c], ps[:, bank + 2 * t + h, :], g_row[:, c], ALU.mult)
                dve.drain()
                for t in range(TT):
                    dve.scalar_tensor_tensor(z_ln[:, t, :], x_sb[:, t, :], ALPHA, z_ln[:, t, :], ALU.mult, ALU.add)
                dve.drain()
                for t in range(TT):
                    for h in range(2):
                        dve.bn_stats(stat[:, t, h, :], z_ln[:, t, 512 * h:512 * h + 512])
                dve.drain()
                for t in range(TT):
                    dve.bn_aggr(mv[:, t, :], stat[:, t].rearrange("p a b -> p (a b)"))
                dve.drain()
                dve.tensor_scalar(v_eps[:], mv[:, :, 1], EPS, None, ALU.add).then_inc(var_ready.sem, 1)
                dve.wait_ge(std_ready.sem, std_ready.at(l, which + 1))
                dve.reciprocal(rinv[:], std[:])
                dve.drain()
                dve.tensor_tensor(newt[:], rinv[:], rinv[:], ALU.mult)
                dve.drain()
                dve.tensor_tensor(newt[:], newt[:], v_eps[:], ALU.mult)
                dve.drain()
                dve.tensor_scalar(newt[:], newt[:], -0.5, 1.5, ALU.mult, ALU.add)
                dve.drain()
                dve.tensor_tensor(rinv[:], rinv[:], newt[:], ALU.mult)
                dve.drain()
                dve.scalar_tensor_tensor(nbias[:], mv[:, :, 0], -1.0, rinv[:], ALU.mult, ALU.mult).then_inc(shift_ready.sem, 1)
                dve.wait_ge(ln_loaded.sem, ln_loaded.at(l, 32 * which + 32))
                for t in range(TT):
                    dve.wait_ge(normed.sem, normed.at(l, 2 * which + t + 1))
                    dve.tensor_tensor(x_sb[:, t, :], x_sb[:, t, :], ln_row[:, 0, :], ALU.mult)
                dve.drain()
                for t in range(TT):
                    d = dve.tensor_tensor(x_sb[:, t, :], x_sb[:, t, :], ln_row[:, 1, :], ALU.add)
                d.then_inc(x_ready.sem, 1)

            def rotate(l, c):
                cs = 0 if c < 4 else 2
                dve.wait_ge(perm_done.sem, perm_done.at(l, c + 1))
                dve.tensor_tensor(rope_t[:, 0, :], qk_raw[:, c, :], rope[:, cs, :], ALU.mult)
                dve.tensor_tensor(rope_t[:, 1, :], ps[:, 7, 0:T], rope[:, cs + 1, :], ALU.mult)
                dve.drain()
                dve.tensor_tensor(qk[:, c, :], rope_t[:, 0, :], rope_t[:, 1, :], ALU.add).then_inc(rope_done.sem, 1)

            def attend(l, n):
                if n < 16:
                    w = 2 * (n // HEADS + 1) * P
                    dve.wait_ge(scored.sem, scored.at(l, n + 1))
                    dve.tensor_reduce(nmax[:, n, :], ps[:, 2 + n % 2, 0:w].rearrange("p (b k) -> p b k", b=2), AX, ALU.max,
                                      negate=True).then_inc(maxed.sem, 1)
                if 1 <= n <= 16:
                    u = n - 1
                    t, h = u // HEADS, u % HEADS
                    w = (t + 1) * P
                    dve.wait_ge(exped.sem, exped.at(l, u + 1))
                    dve.reciprocal(rsum[:, u, :], rsum[:, u, :])
                    dve.drain()
                    dve.tensor_tensor(rsum[:, u, :], rsum[:, u, :], gate3[:, t, 3 * h + 1:3 * h + 3], ALU.mult)
                    dve.drain()
                    for b in range(2):
                        d = dve.tensor_scalar(prob[:, u % 2, b * w:(b + 1) * w], prob[:, u % 2, b * w:(b + 1) * w],
                                              rsum[:, u, b:b + 1], None, ALU.mult)
                    d.then_inc(prob_ready.sem, 1)
                if n in (10, 17):
                    t = n // 16
                    dve.wait_ge(o_hi.sem, o_hi.at(l, t + 1))
                    tc = slice(t * P, (t + 1) * P)
                    dve.tensor_tensor(act1_lo[:, 0:HPG, tc], ps[:, 6 + t, :].rearrange("p (c t) -> p c t", c=HPG),
                                      act1_hi[:, 0:HPG, tc].bitcast(F32), ALU.subtract).then_inc(o_ready.sem, 1)

            dve.wait_ge(start_loaded.sem, 80)
            dve.tensor_copy(bfc[:], bf_stage[:])
            dve.wait_ge(c_exp.sem, 1)
            dve.tensor_scalar(c_silu[:], c_silu[:], 1.0, None, ALU.add)
            dve.drain()
            dve.reciprocal(c_silu[:], c_silu[:])
            dve.drain()
            dve.tensor_tensor(c_silu[:], c_silu[:], raw[:, 0, :], ALU.mult)
            dve.drain().then_inc(raw_done.sem, RING)
            with dve.Fori(0, N_ADA // RING) as j:
                for r in range(RING):
                    dve.wait_ge(raw_loaded[r].sem, 16 * j + 16)
                    dve.tensor_tensor_reduce(raw[:, r, :], raw[:, r, :], c_silu[:], 1.0, 0.0, ALU.mult, ALU.add,
                                             acc4[:, r:r + 1]).then_inc(raw_done.sem, 1)
                dve.drain()
                dve.tensor_tensor(mods[:, bass.ds(RING * j, RING)], mods[:, bass.ds(RING * j, RING)], acc4[:], ALU.add)
                dve.drain()
            m6 = mods[:].rearrange("p (l s j k) -> p l s j k", l=L, s=2, j=3)
            for l in range(L):
                dve.tensor_scalar(m6[:, l, :, 1, :], m6[:, l, :, 1, :], 1.0, None, ALU.add)
                dve.tensor_scalar(m6[:, l, 0, 2, :], m6[:, l, 0, 2, :], 0.5, None, ALU.mult)
            dve.drain().then_inc(x_ready.sem, 1)

            with dve.Fori(0, L) as l:
                for i in range(AHEAD):
                    lo(l, 0, i)
                dve.tensor_copy(mods_l[:], mods[:, bass.ds(l * ADA, ADA)]).then_inc(mods_ready.sem, 1)
                dve.memset(hid_k[:], 0.0)
                dve.memset(hid_v[:], 0.0).then_inc(hid_zero.sem, 1)
                build_h(l, 0, act0_hi, act0_lo)
                dve.wait_ge(params_loaded.sem, params_loaded.at(l, 32))
                for s in range(S_PROJ):
                    lo(l, 0, s + AHEAD)
                    if 2 <= s <= 7:
                        rotate(l, s - 2)
                    if s == 8:
                        for a in range(2):
                            dve.wait_ge(proj_out.sem, proj_out.at(l, 7 + a))
                            for h in range(2):
                                d = dve.tensor_tensor(zpe[:, a, h, :].rearrange("p (n c) -> p n c", c=CMP_STRIDE),
                                                      qk_raw[:, 6 + a, :].rearrange("p (n c) -> p n c", c=CMP_STRIDE),
                                                      cmp_pe[:, a, h * CMP_STRIDE:(h + 1) * CMP_STRIDE].unsqueeze(1)
                                                      .to_broadcast([P, T // CMP_STRIDE, CMP_STRIDE]), ALU.add)
                            d.then_inc(zpe_done.sem, 1)
                    if s == 11:
                        dve.wait_ge(proj_out.sem, proj_out.at(l, 11))
                        dve.tensor_scalar(gate3[:], gate3[:], 0.5, 0.5, ALU.mult, ALU.add)
                        dve.wait_ge(cmp_kv.sem, cmp_kv.at(l, 1))
                        dve.tensor_copy(kc_raw[:], ps[:, 6, 2 * CP:3 * CP]).then_inc(cmp_kraw.sem, 1)
                        dve.tensor_tensor(vc_sel[:], ps[:, 6, P:2 * P].unsqueeze(1).to_broadcast([P, HPG, P]), vsel, ALU.mult).then_inc(cmp_vsel.sem, 1)
                    if s == 12:
                        dve.wait_ge(perm_done.sem, perm_done.at(l, 7))
                        dve.tensor_tensor(kc_t1[:], kc_raw[:], crope[:, 0, :], ALU.mult)
                        dve.tensor_tensor(kc_rot[:], ps[:, 7, 0:CP], crope[:, 1, :], ALU.mult)
                        dve.drain()
                        dve.tensor_tensor(kc_rot[:], kc_rot[:], kc_t1[:], ALU.add).then_inc(rope_done.sem, 1)
                    if s == 14:
                        dve.wait_ge(cmp_scored.sem, cmp_scored.at(l, 1))
                        for t in range(TT):
                            for g in range(GROUPS):
                                sc = ps[:, 6 + g, T + t * HPG * CP:T + (t + 1) * HPG * CP].rearrange("p (h c) -> p h c", c=CP)
                                dve.tensor_tensor(pc[:, t, g * HPG:(g + 1) * HPG], sc, cmask[:, t, :].unsqueeze(1).to_broadcast([P, HPG, CP]), ALU.add)
                        dve.drain()
                        dve.tensor_reduce(pc_m[:].rearrange("p a h -> p (a h)"), pc[:].rearrange("p a h c -> p (a h) c"), AX, ALU.max)
                        dve.drain()
                        dve.tensor_tensor(pc[:].rearrange("p a h c -> p (a h) c"), pc[:].rearrange("p a h c -> p (a h) c"),
                                          pc_m[:].rearrange("p a h -> p (a h)").unsqueeze(2).to_broadcast([P, TT * HEADS, CP]),
                                          ALU.subtract).then_inc(cmp_shift.sem, 1)
                    if s == 15:
                        dve.wait_ge(cmp_exp.sem, cmp_exp.at(l, 1))
                        dve.tensor_reduce(pc_m[:].rearrange("p a h -> p (a h)"), pc[:].rearrange("p a h c -> p (a h) c"), AX, ALU.add)
                        dve.drain()
                        dve.reciprocal(pc_m[:], pc_m[:])
                        dve.drain()
                        for t in range(TT):
                            dve.scalar_tensor_tensor(pc_m[:, t, :], pc_m[:, t, :], any_vis[:, t:t + 1],
                                                     gate3[:, t, :].rearrange("p (h b) -> p b h", b=3)[:, 0, :], ALU.mult, ALU.mult)
                        dve.drain()
                        dve.tensor_tensor(pc[:].rearrange("p a h c -> p (a h) c"), pc[:].rearrange("p a h c -> p (a h) c"),
                                          pc_m[:].rearrange("p a h -> p (a h)").unsqueeze(2).to_broadcast([P, TT * HEADS, CP]),
                                          ALU.mult).then_inc(cmp_prob.sem, 1)
                    if s >= 15:
                        attend(l, s - 15)
                attend(l, 16)
                attend(l, 17)
                for n in range(2):
                    dve.wait_ge(pool_hi.sem, pool_hi.at(l, n + 1))
                    dve.tensor_tensor(act1_lo[:, 4 + 2 * n:6 + 2 * n, :], opf[:, 2 * n:2 * n + 2, :],
                                      act1_hi[:, 4 + 2 * n:6 + 2 * n, :].bitcast(F32), ALU.subtract).then_inc(pool_ready.sem, 1)
                def merge_lo(k):
                    dve.wait_ge(merged_hi.sem, merged_hi.at(l, k + 1))
                    dve.tensor_tensor(act0_lo[:, k, :], mf[:, k % 2, :], act0_hi[:, k, :].bitcast(F32), ALU.subtract).then_inc(merged_ready.sem, 1)

                for k in range(KT):
                    s = S_LIFT + k
                    lo(l, 0, s + AHEAD)
                    dve.wait_ge(slot_used.sem, slot_used.at(l, s + 1))
                    dve.scalar_tensor_tensor(prod[:, k % 2], gab[:, k], 1.0, ps[:, k % 2, :].rearrange("p (a t) -> p a t", a=2),
                                             ALU.add, ALU.mult).then_inc(lift_read.sem, 1)
                    dve.drain()
                    dve.tensor_tensor(mf[:, k % 2, :], prod[:, k % 2, 0, :], prod[:, k % 2, 1, :], ALU.add).then_inc(merged.sem, 1)
                    if k:
                        merge_lo(k - 1)
                merge_lo(KT - 1)
                gate_diag(l, 0)
                for k in range(KT):
                    lo(l, 0, S_OUT + k + AHEAD)
                norm(l, 0, 2, S_OUT + KT - 1)
                build_h(l, 1, act1_hi, act1_lo)
                for k in range(PH):
                    lo(l, 0, S_QUERY + k + AHEAD)
                    dve.wait_ge(q_hi_out.sem, q_hi_out.at(l, k + 1))
                    dve.tensor_tensor(q_lo[:, k, :], ps[:, (S_QUERY + k) % 2, 0:T], q_hi[:, k, :].bitcast(F32), ALU.subtract).then_inc(q_ready.sem, 1)
                dve.wait_ge(scores_out.sem, scores_out.at(l, PH))
                lo(l, 0, S_KEYS + AHEAD)

                def best16(vals, idx, src, rest, between):
                    n = len(src)
                    for p in range(n):
                        dve.max(vals[p][:, 0:8], src[p])
                    dve.drain()
                    for p in range(n):
                        dve.match_replace(rest[p], vals[p][:, 0:8], src[p], -3e38)
                        dve.max_index(idx[p][:, 0:8], vals[p][:, 0:8], src[p])
                    between()
                    dve.drain()
                    for p in range(n):
                        dve.max(vals[p][:, 8:16], rest[p])
                    dve.drain()
                    for p in range(n):
                        dve.max_index(idx[p][:, 8:16], vals[p][:, 8:16], rest[p])

                with dve.Fori(0, 16) as i:
                    j = i + S_UP // RING
                    lo(l, j, AHEAD)
                    dve.tensor_copy(work_s[:], scores[:, bass.ds(i, 1)].rearrange("p u h k -> p (u h) k"))
                    dve.drain()
                    best16([half_v[:, 0, :], half_v[:, 1, :]], [ij_s[:, 0, :], ij_s[:, 1, :]],
                           [work_s[:, 0, :], work_s[:, 1, :]], [work[:, 0, :], work[:, 1, :]],
                           lambda: lo(l, j, AHEAD + 1))
                    dve.tensor_tensor(cand[:], half_v[:, 0, :].unsqueeze(2).to_broadcast([P, TOPK, TOPK]),
                                      half_v[:, 1, :].unsqueeze(1).to_broadcast([P, TOPK, TOPK]), ALU.add)
                    lo(l, j, AHEAD + 2)
                    dve.drain()
                    best16([sv_s[:]], [ci_s[:]], [cand[:].rearrange("p a b -> p (a b)")],
                           [cand2[:].rearrange("p a b -> p (a b)")], lambda: lo(l, j, AHEAD + 3))
                    dve.drain()
                    dve.tensor_copy(sv[:, bass.ds(i, 1), :], sv_s[:].unsqueeze(1))
                    dve.tensor_copy(ci[:, bass.ds(i, 1), :], ci_s[:].unsqueeze(1))
                    dve.tensor_copy(ij[:, bass.ds(i, 1)], ij_s[:].unsqueeze(1))
                    dve.drain()

                with dve.Fori(16, 24) as i:
                    j = i + S_UP // RING
                    for w in range(2):
                        u = 2 * i + (w - 32)
                        lo(l, j, AHEAD + 2 * w)
                        dve.tensor_scalar(ab[:, 0, :], ci[:, bass.ds(u, 1), :].rearrange("p a k -> p (a k)"), 4, None, ALU.logical_shift_right)
                        dve.tensor_scalar(ab[:, 1, :], ci[:, bass.ds(u, 1), :].rearrange("p a k -> p (a k)"), TOPK - 1, None, ALU.bitwise_and)
                        dve.tensor_copy(ij_f[:], ij[:, bass.ds(u, 1)].rearrange("p a h k -> p (a h) k"))
                        dve.drain()
                        for h in range(2):
                            dve.tensor_tensor(onehot[:, h], ab[:, h, :].unsqueeze(2).to_broadcast([P, TOPK, TOPK]),
                                              iota[:, 0:TOPK].unsqueeze(1).to_broadcast([P, TOPK, TOPK]), ALU.is_equal)
                        lo(l, j, AHEAD + 2 * w + 1)
                        dve.drain()
                        for h in range(2):
                            dve.tensor_tensor(onehot[:, h], onehot[:, h], ij_f[:, h, :].unsqueeze(1).to_broadcast([P, TOPK, TOPK]), ALU.mult)
                        dve.drain()
                        for h in range(2):
                            dve.tensor_reduce(sel[:, h, bass.ds(TOPK * u, TOPK)], onehot[:, h], AX, ALU.add)
                dve.drain()
                dve.tensor_copy(rsm[:], sv[:, :, 0])
                dve.drain()
                dve.tensor_tensor(sv[:], sv[:], rsm[:].unsqueeze(2).to_broadcast([P, 2 * PH, TOPK]), ALU.subtract).then_inc(sel_shift.sem, 1)
                dve.wait_ge(sel_exp.sem, sel_exp.at(l, 1))
                dve.tensor_reduce(rsm[:], sv[:], AX, ALU.add)
                dve.drain()
                dve.reciprocal(rsm[:], rsm[:])
                dve.drain()
                dve.tensor_tensor(sel[:, 2, :].rearrange("p (u k) -> p u k", k=TOPK), sv[:],
                                  rsm[:].unsqueeze(2).to_broadcast([P, 2 * PH, TOPK]), ALU.mult).then_inc(routed.sem, 1)
                with dve.Fori(24, 32) as i:
                    for n in range(RING):
                        lo(l, i + S_UP // RING, n + AHEAD)
                dve.wait_ge(sel_out.sem, sel_out.at(l, 1))

                def weighted(k, b):
                    for t in range(4):
                        tok = 4 * k + t
                        d = dve.tensor_scalar(oh1g[:, b, t, :], iota, sel[:, 0, bass.ds(tok, 1)], sel[:, 2, bass.ds(tok, 1)],
                                              ALU.is_equal, ALU.mult)
                    d.then_inc(oh1_ready.sem, 1)

                def apply_gates(k, b):
                    dve.wait_ge(gates_done.sem, gates_done.at(l, k + 1))
                    e = experts[:, :, bass.ds(4 * k, 4)].rearrange("p i t -> p t i")
                    dve.tensor_tensor(e, e, ps[:, 2 + b, :].rearrange("p (t i) -> p t i", t=4), ALU.mult).then_inc(gates_applied.sem, 1)

                for b in range(2):
                    weighted(b, b)
                with dve.Fori(0, T // 8 - 1) as i:
                    for b in range(2):
                        apply_gates(2 * i + b, b)
                        weighted(2 * i + (b + 2), b)
                for b in range(2):
                    apply_gates(T // 4 - 2 + b, b)

                def gated(i, b):
                    dve.wait_ge(g_hi_out.sem, g_hi_out.at(l, i + 1))
                    dve.tensor_tensor(g_lo[:, b].rearrange("p a t -> p (a t)"), experts[:, bass.ds(RING * i, RING), :].rearrange("p a t -> p (a t)"),
                                      g_hi[:, b].rearrange("p a t -> p (a t)").bitcast(F32), ALU.subtract).then_inc(g_ready.sem, 1)

                def down(i, b, more=True):
                    lo(l, i + S_DOWN // RING, AHEAD)
                    if more:
                        gated(i + 1, b)
                        for n in range(1, RING):
                            lo(l, i + S_DOWN // RING, n + AHEAD)

                gated(0, 0)
                down(0, 1)
                with dve.Fori(0, 15) as h:
                    down(2 * h + 1, 0)
                    down(2 * h + 2, 1)
                down(NK // 4 - 1, None, more=False)
                gate_diag(l, 1)
                norm(l, 1, 4, SLOTS - 1)

        @block.tensor
        def _(pe):
            mm = pe.matmul

            def split_ready(l, j, i):
                pe.wait_ge(raw_done.sem, raw_done.at(l, RING * j + (i + 1)))

            def turn_x(l, which, banks):
                pe.wait_ge(x_ready.sem, x_ready.at(l, which))
                for k in range(KT):
                    for t in range(TT):
                        m = pe.transpose(ps[:, banks + k // 2, (k % 2) * T + t * P:(k % 2) * T + (t + 1) * P],
                                         x_sb[:, t, k * P:(k + 1) * P], ident)
                    if k % 2:
                        m.then_inc(xt_done.sem, 1)

            def by_features(dst, r, a_hi, a_lo, kts, w_at=0):
                n = len(kts)
                for q, k in enumerate(kts):
                    wc = slice((w_at + q) * P, (w_at + q + 1) * P)
                    mm(dst, w_hi[:, r, wc], a_hi[:, k, :], start=(q == 0), stop=False)
                    mm(dst, w_hi[:, r, wc], a_lo[:, k, :], start=False, stop=False)
                    m = mm(dst, w_lo[:, r, wc], a_hi[:, k, :], start=False, stop=(q == n - 1))
                return m

            def by_tokens(bank, r):
                for t in range(TT):
                    tc = slice(t * P, (t + 1) * P)
                    dst = ps[:, bank, t * P:(t + 1) * P]
                    for k in range(KT):
                        wc = slice(k * P, (k + 1) * P)
                        mm(dst, act0_hi[:, k, tc], w_hi[:, r, wc], start=(k == 0), stop=False)
                        mm(dst, act0_hi[:, k, tc], w_lo[:, r, wc], start=False, stop=False)
                        m = mm(dst, act0_lo[:, k, tc], w_hi[:, r, wc], start=False, stop=(k == KT - 1))
                return m

            def spread_gate(l, which, bank):
                pe.wait_ge(diag_ready.sem, diag_ready.at(l, which + 1))
                for k in range(KT):
                    m = mm(ps[:, bank + k // 4, (k % 4) * P:(k % 4 + 1) * P], ones, diag[:, k, :], start=True, stop=True)
                m.then_inc(gate_spread.sem, 1)

            def head(u):
                t, h = u // HEADS, u % HEADS
                return t, h % HPG, h // HPG, (h // HPG) * HD

            def score(l, u):
                t, c, g, p0 = head(u)
                n = (t + 1) * P
                if u >= 2:
                    pe.wait_ge(exped.sem, exped.at(l, u - 1))
                for b in range(2):
                    dst = ps[:, 2 + u % 2, b * n:(b + 1) * n]
                    mm(dst, qk[p0:p0 + HD, c, t * P:(t + 1) * P], qk[p0:p0 + HD, 4 + b, 0:n], start=True, stop=False)
                    m = mm(ps[:, 2 + u % 2, b * n + t * P:(b + 1) * n], ident_bf, mask_bf, start=False, stop=True)
                m.then_inc(scored.sem, 1)

            def turn_prob(l, u):
                t = u // HEADS
                pe.wait_ge(prob_ready.sem, prob_ready.at(l, u + 1))
                if u >= 2:
                    pe.wait_ge(pt_out.sem, pt_out.at(l, u - 1))
                for k in range(2 * (t + 1)):
                    m = pe.transpose(ps[:, 4 + u % 2, k * P:(k + 1) * P], prob[:, u % 2, k * P:(k + 1) * P], ident)
                m.then_inc(turned.sem, 1)

            def mix_values(l, u):
                t, c, g, p0 = head(u)
                bank = 6 + t
                if u % HEADS == 0:
                    pe.wait_ge(cmp_pt.sem, cmp_pt.at(l, 1))
                    pe.wait_ge(cmp_vsel.sem, cmp_vsel.at(l, 1))
                    for k in range(HPG):
                        mm(ps[:, bank, k * P:(k + 1) * P], vc_sel[:, k, :], pc_t[:, t, :], start=(k == 0), stop=False, skip_group_check=True)
                pe.wait_ge(pt_out.sem, pt_out.at(l, u + 1))
                for b in range(2):
                    for k in range(t + 1):
                        m = mm(ps[p0:p0 + HD, bank, c * P:(c + 1) * P], vtok[:, b, k * P + g * HD:k * P + (g + 1) * HD],
                               prob_t[:, u % 2, (b * (t + 1) + k) * P:(b * (t + 1) + k + 1) * P], start=False,
                               stop=(u % HEADS == HEADS - 1 and b == 1 and k == t), skip_group_check=True)
                m.then_inc(pv_done.sem, 1)

            pe.drain().then_inc(slot_used.sem, RING)
            pe.wait_ge(start_loaded.sem, 80)
            with pe.Fori(0, L) as l:
                turn_x(l, 0, 2)
                pe.wait_ge(h_ready.sem, h_ready.at(l, 2))
                for s in range(S_PROJ):
                    if s >= 15:
                        if s == 15:
                            pe.wait_ge(rope_done.sem, rope_done.at(l, 7))
                        score(l, s - 15)
                    split_ready(l, 0, s)
                    if s >= 2:
                        pe.wait_ge(proj_out.sem, proj_out.at(l, s - 1))
                    if 8 <= s <= 10:
                        m = by_tokens(s % 2, s % RING)
                    else:
                        m = by_features(ps[:, s % 2, 0:T], s % RING, act0_hi, act0_lo, range(KT))
                    m.then_inc(slot_used.sem, 1)
                    if 1 <= s <= 6:
                        c = s - 1
                        pe.wait_ge(proj_out.sem, proj_out.at(l, c + 1))
                        if c:
                            pe.wait_ge(rope_done.sem, rope_done.at(l, c))
                        mm(ps[:, 7, 0:T], perm, qk_raw[:, c, :], start=True, stop=True).then_inc(perm_done.sem, 1)
                    if s == 8:
                        for a in range(2):
                            pe.wait_ge(zpe_done.sem, zpe_done.at(l, a + 1))
                            for n in range(CMP_LEN):
                                src = zpe[:, a, n // CMP_STRIDE, :].rearrange("p (n c) -> p c n", c=CMP_STRIDE)
                                n0 = n // CMP_STRIDE
                                m = mm(ps[:, 6, a * CP:a * CP + N_CMP], cmp_w1[:, a, n, :], src[:, n % CMP_STRIDE, n0:n0 + N_CMP],
                                       start=(n == 0), stop=(n == CMP_LEN - 1))
                        m.then_inc(cmp_hid.sem, 1)
                    if s == 10:
                        pe.wait_ge(cmp_gelu.sem, cmp_gelu.at(l, 1))
                        mm(ps[:, 6, 2 * CP:3 * CP], cmp_w2[:, 0, :], hid_k[:], start=True, stop=True)
                        mm(ps[:, 6, P:2 * P], hid_v[:].rearrange("p h c -> p (h c)"), cmp_w2[:, 1, :], start=True, stop=True).then_inc(cmp_kv.sem, 1)
                    if s == 11:
                        pe.wait_ge(cmp_kraw.sem, cmp_kraw.at(l, 1))
                        pe.wait_ge(rope_done.sem, rope_done.at(l, 6))
                        mm(ps[:, 7, 0:CP], perm, kc_raw[:], start=True, stop=True).then_inc(perm_done.sem, 1)
                    if s == 13:
                        pe.wait_ge(rope_done.sem, rope_done.at(l, 7))
                        pe.wait_ge(cmp_vsel.sem, cmp_vsel.at(l, 1))
                        for u in range(2 * HEADS):
                            t, c, g, p0 = head(u)
                            at = T + (t * HPG + c) * CP
                            m = mm(ps[:, 6 + g, at:at + CP], qk[p0:p0 + HD, c, t * P:(t + 1) * P], kc_rot[p0:p0 + HD, :], start=True, stop=True)
                        m.then_inc(cmp_scored.sem, 1)
                    if s == 15:
                        pe.wait_ge(cmp_prob.sem, cmp_prob.at(l, 1))
                        for t in range(TT):
                            m = pe.transpose(ps[:, 7, t * P:(t + 1) * P], pc[:, t].rearrange("p h c -> p (h c)"), ident)
                        m.then_inc(cmp_turned.sem, 1)
                    if s >= 16:
                        turn_prob(l, s - 16)
                    if s >= 17:
                        mix_values(l, s - 17)
                turn_prob(l, 15)
                mix_values(l, 14)
                mix_values(l, 15)
                for n in range(2):
                    pe.wait_ge(exped.sem, exped.at(l, 15 + n))
                    pe.wait_ge(pooled_ready.sem, pooled_ready.at(l, 2 * n + 2))
                    for g in (2 * n, 2 * n + 1):
                        m = mm(ps[:, 2 + n, (g % 2) * T:(g % 2 + 1) * T], w_pool[:, g, :], pooled[:, g, :], start=True, stop=True)
                    m.then_inc(pool_mixed.sem, 1)
                pe.wait_ge(o_ready.sem, o_ready.at(l, 2))
                pe.wait_ge(pool_ready.sem, pool_ready.at(l, 2))
                for k in range(KT):
                    s = S_LIFT + k
                    split_ready(l, 0, s)
                    if k < 2:
                        pe.wait_ge(proj_out.sem, proj_out.at(l, S_PROJ))
                    else:
                        pe.wait_ge(lift_read.sem, lift_read.at(l, k - 1))
                    by_features(ps[:, k % 2, 0:T], s % RING, act1_hi, act1_lo, range(0, 4))
                    by_features(ps[:, k % 2, T:2 * T], s % RING, act1_hi, act1_lo, range(4, 8), w_at=4).then_inc(slot_used.sem, 1)
                spread_gate(l, 0, 6)
                for k in range(KT):
                    s = S_OUT + k
                    split_ready(l, 0, s)
                    pe.wait_ge(merged_ready.sem, merged_ready.at(l, k + 1))
                    for t in range(TT):
                        tc = slice(t * P, (t + 1) * P)
                        for h in range(2):
                            wc = slice(512 * h, 512 * h + 512)
                            dst = ps[:, 2 + 2 * t + h, :]
                            mm(dst, act0_hi[:, k, tc], w_hi[:, s % RING, wc], start=(k == 0), stop=False)
                            mm(dst, act0_hi[:, k, tc], w_lo[:, s % RING, wc], start=False, stop=False)
                            m = mm(dst, act0_lo[:, k, tc], w_hi[:, s % RING, wc], start=False, stop=(k == KT - 1))
                    m.then_inc(slot_used.sem, 1)
                turn_x(l, 1, 2)
                pe.wait_ge(h_ready.sem, h_ready.at(l, 4))
                for k in range(PH):
                    s = S_QUERY + k
                    split_ready(l, 0, s)
                    if k >= 2:
                        pe.wait_ge(q_ready.sem, q_ready.at(l, k - 1))
                    by_features(ps[:, s % 2, 0:T], s % RING, act1_hi, act1_lo, range(KT)).then_inc(slot_used.sem, 1)
                split_ready(l, 0, S_KEYS)
                pe.wait_ge(q_ready.sem, q_ready.at(l, PH))
                r = S_KEYS % RING
                for k in range(PH):
                    if k >= 2:
                        pe.wait_ge(scores_out.sem, scores_out.at(l, k - 1))
                    for v in range(2):
                        t, h = (2 * k + v) // PH, (2 * k + v) % PH
                        tc, wc = slice(t * P, (t + 1) * P), slice(h * P, (h + 1) * P)
                        for p in range(2):
                            pp = slice(p * HD, (p + 1) * HD)
                            dst = ps[:, 2 + 2 * (k % 2) + p, v * NK:(v + 1) * NK]
                            mm(dst, q_hi[pp, h, tc], w_hi[pp, r, wc], start=True, stop=False)
                            mm(dst, q_hi[pp, h, tc], w_lo[pp, r, wc], start=False, stop=False)
                            m = mm(dst, q_lo[pp, h, tc], w_hi[pp, r, wc], start=False, stop=True)
                    m.then_inc(keys_scored.sem if k < PH - 1 else slot_used.sem, 1)

                def up(i, first):
                    for n in range(RING):
                        split_ready(l, i + S_UP // RING, n)
                        if not (first and n < 2):
                            pe.wait_ge(gelu_done.sem, gelu_done.at(l, RING * i + (n - 1)))
                        by_features(ps[:, n % 2, 0:T], n, act1_hi, act1_lo, range(KT)).then_inc(slot_used.sem, 1)

                up(0, True)
                with pe.Fori(1, NK // RING) as i:
                    up(i, False)
                pe.wait_ge(routed.sem, routed.at(l, 1))
                for a in range(3):
                    for t in range(TT):
                        at = a * T + t * P
                        m = pe.transpose(ps[:, 2 + at // 512, at % 512:at % 512 + P], sel[:, a, t * P:(t + 1) * P], ident)
                m.then_inc(sel_turned.sem, 1)

                def gates(k, b, first):
                    pe.wait_ge(oh2_ready.sem, oh2_ready.at(l, k + 1))
                    pe.wait_ge(oh1_ready.sem, oh1_ready.at(l, k + 1))
                    if first:
                        pe.wait_ge(sel_out.sem, sel_out.at(l, 1))
                    else:
                        pe.wait_ge(gates_applied.sem, gates_applied.at(l, k - 1))
                    for t in range(4):
                        m = mm(ps[:, 2 + b % 2, t * P:(t + 1) * P], oh2[:, b, t, :], oh1g[:, b % 2, t, :], start=True, stop=True)
                    m.then_inc(gates_done.sem, 1)

                for b in range(4):
                    gates(b, b, b < 2)
                with pe.Fori(1, T // 16) as i:
                    for b in range(4):
                        gates(4 * i + b, b, False)

                def down(i, b, first=False, last=False):
                    pe.wait_ge(g_ready.sem, g_ready.at(l, i + 1))
                    for n in range(RING):
                        split_ready(l, i + S_DOWN // RING, n)
                        for t in range(TT):
                            tc = slice(t * P, (t + 1) * P)
                            for h in range(2):
                                wc = slice(512 * h, 512 * h + 512)
                                dst = ps[:, 4 + 2 * t + h, :]
                                mm(dst, g_hi[:, b, n, tc], w_hi[:, n, wc], start=(first and n == 0), stop=False, skip_group_check=True)
                                mm(dst, g_hi[:, b, n, tc], w_lo[:, n, wc], start=False, stop=False, skip_group_check=True)
                                m = mm(dst, g_lo[:, b, n, tc], w_hi[:, n, wc], start=False, stop=(last and n == RING - 1), skip_group_check=True)
                        m.then_inc(slot_used.sem, 1)

                down(0, 0, first=True)
                with pe.Fori(0, 15) as h:
                    down(2 * h + 1, 1)
                    down(2 * h + 2, 0)
                down(NK // 4 - 1, 1, last=True)
                spread_gate(l, 1, 2)


def _tables():
    f = np.float32
    keep = np.zeros((P, KEEP), f)
    keep[:, K_IDENT:K_IDENT + P] = np.eye(P, dtype=f)
    half = ROT // 2
    for g in range(GROUPS):
        for i in range(half):
            keep[g * HD + i, K_PERM + g * HD + i + half] = 1
            keep[g * HD + i + half, K_PERM + g * HD + i] = 1
    keep[:, K_IOTA:K_IOTA + P] = np.arange(P, dtype=f)
    keep[:, K_ONES:K_ONES + P] = 1

    def rot(pos):
        inv = f(500000.0) ** (-np.arange(0, ROT, 2, dtype=f) / f(ROT))
        ang = pos.astype(f)[:, None] * inv[None, :].astype(f)
        c, s = np.ones((P, len(pos)), f), np.zeros((P, len(pos)), f)
        for g in range(GROUPS):
            for i in range(half):
                a, b = g * HD + i, g * HD + i + half
                c[a] = c[b] = np.cos(ang[:, i])
                s[a], s[b] = -np.sin(ang[:, i]), np.sin(ang[:, i])
        return c, s

    mix = np.zeros((P, MIX), f)
    c, s = rot(np.arange(T))
    mix[:, M_ROPE:M_CROPE] = np.concatenate([c * f(SCALE), s * f(SCALE), c, s], 1)
    c, s = rot(np.arange(N_CMP) * CMP_STRIDE + CMP_LEN - 1)
    mix[:, M_CROPE:M_CROPE + N_CMP] = c
    mix[:, M_CROPE + CP:M_CROPE + CP + N_CMP] = s
    end = np.arange(CP) * CMP_STRIDE + CMP_LEN - 1
    for t in range(TT):
        tok = t * P + np.arange(P)
        vis = (end[None, :] <= tok[:, None]) & (np.arange(CP) < N_CMP)[None, :]
        mix[:, M_CMASK + t * CP:M_CMASK + (t + 1) * CP] = np.where(vis, 0, NEG)
        mix[:, M_ANY + t] = vis.any(1)
    for h in range(HPG):
        for g in range(GROUPS):
            r = (g * HPG + h) * CP
            mix[r:r + CP, M_VSEL + h * P + g * HD:M_VSEL + h * P + (g + 1) * HD] = 1
    for g, w in enumerate(POOL_W):
        mix[:, M_CNT + g * T:M_CNT + (g + 1) * T] = f(1) / np.minimum(np.arange(T) + 1, w).astype(f)
    bf = np.zeros((P, 2 * P), f)
    bf[:, :P] = np.eye(P)
    bf[:, P:] = np.where(np.arange(P)[None, :] <= np.arange(P)[:, None], 0, NEG)
    return keep, mix, bf


def _layout(c, w_ada, b_ada, w_in, cmp_pe, cmp_w1, cmp_w2, w_pool, pool_scale, w_lift, w_o, ln_g, ln_b,
            peer_wq, peer_keys, peer_u, peer_v):
    stream = np.zeros((N_ADA + L * SLOTS, P, D), np.float32)
    att, kvw = HEADS * HD, 6 * GROUPS * HD
    order = []
    for h in range(HPG):
        for g in range(GROUPS):
            order += list(range((g * HPG + h) * HD, (g * HPG + h + 1) * HD))
    by_pairs = list(order)
    kv = lambda branch, kind: list(range(att + (branch * 2 + kind) * P, att + (branch * 2 + kind + 1) * P))
    order += kv(1, 0) + kv(2, 0) + kv(0, 0) + kv(0, 1) + kv(1, 1) + kv(2, 1)
    gates = list(range(att + kvw, att + kvw + 24))
    rest = list(range(att + kvw + 24, w_in.shape[2]))

    def tiles(w):
        k, n = w.shape
        return w.reshape(k // P, P, n // P, P).transpose(2, 1, 0, 3).reshape(n // P, P, (k // P) * P)

    pack = np.zeros((L, P, PACK), np.float32)
    for l in range(L):
        stream[l * ADA:(l + 1) * ADA] = w_ada[l].T.reshape(ADA, P, D)
        s = stream[N_ADA + l * SLOTS:N_ADA + (l + 1) * SLOTS]
        s[0:10] = tiles(w_in[l][:, order])
        s[10].reshape(P, KT, P)[:, :, :24] = w_in[l][:, gates].reshape(KT, P, 24).transpose(1, 0, 2)
        s[11:S_PROJ] = tiles(w_in[l][:, rest])
        s[S_LIFT:S_OUT, :, :512] = tiles(w_lift[l, 0][by_pairs])
        s[S_LIFT:S_OUT, :, 512:] = tiles(w_lift[l, 1])
        s[S_OUT:S_QUERY] = w_o[l].reshape(KT, P, D)
        s[S_QUERY:S_KEYS] = tiles(peer_wq[l])
        s[S_KEYS] = peer_keys[l].transpose(1, 3, 0, 2).reshape(P, D)
        s[S_UP:S_DOWN] = peer_u[l].reshape(NK, P, KT, P).transpose(0, 3, 2, 1).reshape(NK, P, D)
        s[S_DOWN:] = peer_v[l].reshape(NK, P, D)
        p = pack[l]
        w1 = p[:, W_CMP1:W_CMP2].reshape(P, 2, CMP_LEN, P)
        w2 = p[:, W_CMP2:W_PE].reshape(P, 2, P)
        for g in range(GROUPS):
            r = slice(g * HD, (g + 1) * HD)
            w1[r, :, :, r] = cmp_w1[l].reshape(2, CMP_LEN, HD, HD).transpose(2, 0, 1, 3)
            w2[r, :, r] = cmp_w2[l].transpose(1, 0, 2)
            p[r, W_PE:W_POOL] = cmp_pe[l].transpose(2, 0, 1).reshape(HD, 2 * CMP_LEN)
        p[:, W_CMP1:W_CMP2] = w1.reshape(P, -1)
        p[:, W_CMP2:W_PE] = w2.reshape(P, -1)
        p[:, W_POOL:W_PSC] = w_pool[l].transpose(1, 0, 2).reshape(P, POOL_G * P)
        p[:, W_PSC:] = pool_scale[l].reshape(POOL_G, P).T
    ln_gb = np.stack([ln_g[:, 0], ln_b[:, 0], ln_g[:, 1], ln_b[:, 1]], 1).reshape(L, 4, 1, D)
    return stream, np.ascontiguousarray(b_ada.reshape(N_ADA, P).T), pack, np.ascontiguousarray(ln_gb)


def kernel(x, c, w_ada, b_ada, w_in, cmp_pe, cmp_w1, cmp_w2, w_pool, pool_scale, w_lift, w_o,
           ln_g, ln_b, peer_wq, peer_keys, peer_u, peer_v):
    import concourse.bacc as bacc
    from concourse.bass_utils import run_bass_kernel_spmd

    weights = [np.asarray(a) for a in (c, w_ada, b_ada, w_in, cmp_pe, cmp_w1, cmp_w2, w_pool, pool_scale, w_lift,
                                       w_o, ln_g, ln_b, peer_wq, peer_keys, peer_u, peer_v)]
    stream, bias, pack, ln_gb = _layout(*weights)
    keep, mix, bf = _tables()
    arrays = {"in_stream": stream, "in_x": np.ascontiguousarray(x), "in_c": np.ascontiguousarray(c), "in_b_ada": bias,
              "in_pack": pack, "in_ln": ln_gb, "in_keep": keep, "in_mix": mix, "in_bf": bf}
    nc = bacc.Bacc("TRN2", target_bir_lowering=False, num_devices=1)
    aps = [nc.dram_tensor(n, a.shape, mybir.dt.from_np(a.dtype), kind="ExternalInput").ap() for n, a in arrays.items()]
    out = nc.dram_tensor("out_x", (1, T, D), F32, kind="ExternalOutput").ap()
    program(nc, *aps, out)
    r = run_bass_kernel_spmd(nc, [arrays], core_ids=[0])
    return r.results[0]["out_x"]
```

```python
import concourse.bass as bass
from concourse import mybir
import numpy as np

F32 = mybir.dt.float32
F32R = mybir.dt.float32r
BF16 = mybir.dt.bfloat16
U32 = mybir.dt.uint32
ACT = mybir.ActivationFunctionType
ALU = mybir.AluOpType
AX = mybir.AxisListType.X

P = 128
D = 1024
T = 256
L = 2
KT = D // P
TT = T // P
HEADS, HD, GROUPS = 8, 64, 2
HPG = HEADS // GROUPS
CMP_LEN, CMP_STRIDE = 32, 16
N_CMP = (T - CMP_LEN) // CMP_STRIDE + 1
CP = 16
ROT = HD // 4
POOL_G = 4
POOL_W = (2, 4, 8, 16)
PAD = 16
PH, NK, TOPK = 8, 128, 16
SCALE = HD ** -0.5
NEG = -1e30
ALPHA = float((2 * L) ** 0.25)
EPS = 1e-5

RING = 4
ADA = 6 * KT
ADA_PRE = 2 * KT
ADA_LATE = ADA - ADA_PRE
LATE_RING = 3
N_PRE = L * ADA_PRE
S_PROJ = 31
S_LIFT = S_PROJ
S_OUT = S_LIFT + KT
S_QUERY = S_OUT + KT
S_KEYS = S_QUERY + PH
S_UP = S_KEYS + 1
S_DOWN = S_UP + NK
SLOTS = S_DOWN + NK
ROUTE_ROW = 116
AHEAD = 3
LATE_AT = 10
LATE_STEPS = sorted(list(range(LATE_AT, S_PROJ)) + [10, 12, 13]) + list(range(S_QUERY, S_KEYS))
assert len(LATE_STEPS) == ADA_LATE

K_IDENT, K_PERM, K_IOTA, K_ONES, KEEP = 0, P, 2 * P, 3 * P, 4 * P
M_ROPE = 0
M_CROPE = M_ROPE + 4 * T
M_CMASK = M_CROPE + 2 * CP
M_ANY = M_CMASK + TT * CP
M_VSEL = M_ANY + TT
M_CNT = M_VSEL + HPG * P
MIX = M_CNT + POOL_G * T
W_CMP1 = 0
W_CMP2 = W_CMP1 + 2 * CMP_LEN * P
W_PE = W_CMP2 + 2 * P
W_POOL = W_PE + 2 * CMP_LEN
W_PSC = W_POOL + POOL_G * P
PACK = W_PSC + POOL_G


class Signal:

    def __init__(self, nc, name, per_layer, before=0):
        self.sem = nc.alloc_semaphore(name)
        self.per_layer, self.before = per_layer, before

    def at(self, layer, n):
        return layer * self.per_layer + (n + self.before)


def program(nc, stream, late, ln_cols, x_in, c_in, b_ada, pack, ln_gb, const_keep, const_mix, const_bf, out):
    base = (nc.sbuf_base + 63) // 64 * 64
    top = [base]

    def keep(name, shape, dtype=F32, size=4):
        t = nc.alloc_sbuf_tensor_at(name, [P] + shape, dtype, offset=top[0])
        top[0] += (int(np.prod(shape)) * size + 31) // 32 * 32
        return t

    raw = keep("raw", [RING, D])
    w_hi = keep("w_hi", [RING, D], F32R)
    w_lo = keep("w_lo", [RING, D], F32R)
    act_at = top[0]
    act1_hi = keep("act1_hi", [KT, T], F32R)
    act1_lo = keep("act1_lo", [KT, T], F32R)
    x_sb = keep("x_sb", [TT, D])
    kc = keep("kc", [KEEP])
    bfc = keep("bfc", [2 * P], BF16, 2)
    mods = keep("mods", [L * ADA])
    mods_l = keep("mods_l", [ADA])
    acc4 = keep("acc4", [RING])
    stat = keep("stat", [TT, 2, 6])
    mv = keep("mv", [TT, 2])
    v_eps = keep("v_eps", [TT])
    std = keep("std", [TT])
    rinv = keep("rinv", [TT])
    newt = keep("newt", [TT])
    fold = keep("fold", [KT])
    nbias = keep("nbias", [TT])
    acc_late = keep("acc_late", [ADA_LATE])
    lnc = keep("lnc", [2 * L, 2, KT])
    sel_at = top[0]
    c_silu = keep("c_silu", [D])
    sel = nc.alloc_sbuf_tensor_at("sel", [P, 3, T], F32, offset=sel_at)
    oh2 = nc.alloc_sbuf_tensor_at("oh2", [P, 4, 4, P], F32, offset=act_at)
    oh1g = nc.alloc_sbuf_tensor_at("oh1g", [P, 2, 4, P], F32, offset=act_at + 8192)
    g_hi = nc.alloc_sbuf_tensor_at("g_hi", [P, 2, 4, T], F32R, offset=act_at)
    g_lo = nc.alloc_sbuf_tensor_at("g_lo", [P, 2, 4, T], F32R, offset=act_at + 8192)

    big_at = (top[0] + 63) // 64 * 64
    experts = nc.alloc_sbuf_tensor_at("experts", [P, NK, T], F32, offset=big_at)
    off = [0]

    def mix(name, shape, dtype=F32, at=None):
        n = int(np.prod(shape))
        a = off[0] if at is None else at
        if at is None:
            off[0] += (n + 7) // 8 * 8
        assert a + n <= NK * T, (name, a + n)
        return nc.alloc_sbuf_tensor_at(name, [P] + shape, dtype, offset=big_at + 4 * a), a

    act0_hi, _ = mix("act0_hi", [KT, T], F32R)
    act0_lo, _ = mix("act0_lo", [KT, T], F32R)
    hf, hf_at = mix("hf", [KT, T])
    z_ln, _ = mix("z_ln", [TT, D], at=hf_at)
    opf, _ = mix("opf", [POOL_G, T], at=hf_at)
    mf, _ = mix("mf", [2, T], at=hf_at + POOL_G * T)
    wp, wp_at = mix("wp", [PACK])
    cm, _ = mix("cm", [MIX])
    qk_raw, qk_raw_at = mix("qk_raw", [8, T])
    prod, _ = mix("prod", [2, 2, T], at=qk_raw_at)
    qk, _ = mix("qk", [6, T])
    zpe, zpe_at = mix("zpe", [2, 2, T])
    prob_t, _ = mix("prob_t", [2, 2 * T], at=zpe_at)
    vtok, _ = mix("vtok", [2, T])
    gate3, _ = mix("gate3", [TT, 24])
    pin, _ = mix("pin", [POOL_G, PAD + T])
    psum2, _ = mix("psum2", [2, PAD + T])
    pooled, _ = mix("pooled", [POOL_G, T])
    gab, gab_at = mix("gab", [KT, 2, T])
    hid_k, _ = mix("hid_k", [CP])
    hid_v, _ = mix("hid_v", [HEADS, CP])
    hid_t, _ = mix("hid_t", [2, P], at=hf_at)
    kc_raw, _ = mix("kc_raw", [CP])
    kc_t1, _ = mix("kc_t1", [CP])
    kc_rot, _ = mix("kc_rot", [CP])
    vc_sel, _ = mix("vc_sel", [HPG, P])
    pc, _ = mix("pc", [TT, HEADS, CP])
    pc_m, _ = mix("pc_m", [TT, HEADS])
    pc_t, _ = mix("pc_t", [TT, P])
    prob, _ = mix("prob", [2, 2 * T])
    nmax, _ = mix("nmax", [2 * HEADS, 2])
    rsum, _ = mix("rsum", [2 * HEADS, 2])
    rope_t, _ = mix("rope_t", [2, T])
    g_row, _ = mix("g_row", [D], at=qk_raw_at)
    diag, _ = mix("diag", [KT, P], at=qk_raw_at + D)
    ln_row, _ = mix("ln_row", [2, D], at=gab_at)
    LN_END = (gab_at + 2 * D + T - 1) // T
    late_sb, _ = mix("late_sb", [LATE_RING, D], at=wp_at)
    q_hi, _ = mix("q_hi", [PH, T], F32R, at=64 * T)
    q_lo, _ = mix("q_lo", [PH, T], F32R, at=72 * T)
    kb_hi, _ = mix("kb_hi", [PH, 2 * NK], F32R, at=80 * T)
    kb_lo, _ = mix("kb_lo", [PH, 2 * NK], F32R, at=88 * T)
    r_at = (ROUTE_ROW - 2 * PH * 2 * NK // T) * T
    scores, _ = mix("scores", [2 * PH, 2, NK], at=r_at)
    r_at += 2 * PH * 2 * NK
    sv, _ = mix("sv", [2 * PH, TOPK], at=r_at)
    ci, _ = mix("ci", [2 * PH, TOPK], U32, at=r_at + 256)
    ij, _ = mix("ij", [2 * PH, 2, TOPK], U32, at=r_at + 512)
    half_v, _ = mix("half_v", [2, TOPK], at=r_at + 1024)
    work, _ = mix("work", [2, NK], at=r_at + 1056)
    cand, _ = mix("cand", [TOPK, TOPK], at=r_at + 1312)
    cand2, _ = mix("cand2", [TOPK, TOPK], at=r_at + 1568)
    ab, _ = mix("ab", [2, TOPK], U32, at=r_at + 1824)
    onehot, _ = mix("onehot", [2, TOPK, TOPK], at=r_at + 1856)
    rsm, _ = mix("rsm", [2 * PH], at=r_at + 2368)
    work_s, _ = mix("work_s", [2, NK], at=r_at + 2384)
    sv_s, _ = mix("sv_s", [TOPK], at=r_at + 2640)
    ci_s, _ = mix("ci_s", [TOPK], U32, at=r_at + 2656)
    ij_s, _ = mix("ij_s", [2, TOPK], U32, at=r_at + 2672)
    ij_f, _ = mix("ij_f", [2, TOPK], at=r_at + 2704)
    c_tmp, _ = mix("c_tmp", [D], at=0)
    bf_stage, _ = mix("bf_stage", [2 * P], at=D)
    assert top[0] <= big_at and big_at + 4 * NK * T <= nc.sbuf_usable_end, (big_at, nc.sbuf_usable_end)

    ps = nc.alloc_psum_tensor("ps", [P, 8, 512], F32)
    ident, perm = kc[:, K_IDENT:K_IDENT + P], kc[:, K_PERM:K_PERM + P]
    iota, ones = kc[:, K_IOTA:K_IOTA + P], kc[:, K_ONES:K_ONES + P]
    zeros = kc[:, K_PERM + ROT:K_PERM + ROT + PAD]
    ident_bf, mask_bf = bfc[:, 0:P], bfc[:, P:2 * P]
    rope = cm[:, M_ROPE:M_ROPE + 4 * T].rearrange("p (a t) -> p a t", a=4)
    crope = cm[:, M_CROPE:M_CROPE + 2 * CP].rearrange("p (a c) -> p a c", a=2)
    cmask = cm[:, M_CMASK:M_CMASK + TT * CP].rearrange("p (a c) -> p a c", a=TT)
    any_vis = cm[:, M_ANY:M_ANY + TT]
    vsel = cm[:, M_VSEL:M_VSEL + HPG * P].rearrange("p (a c) -> p a c", a=HPG)
    inv_cnt = cm[:, M_CNT:M_CNT + POOL_G * T].rearrange("p (a c) -> p a c", a=POOL_G)
    cmp_w1 = wp[:, W_CMP1:W_CMP2].rearrange("p (a l m) -> p a l m", a=2, l=CMP_LEN)
    cmp_w2 = wp[:, W_CMP2:W_PE].rearrange("p (a m) -> p a m", a=2)
    cmp_pe = wp[:, W_PE:W_POOL].rearrange("p (a l) -> p a l", a=2)
    w_pool = wp[:, W_POOL:W_PSC].rearrange("p (a m) -> p a m", a=POOL_G)
    pool_sc = wp[:, W_PSC:PACK]

    def sig(name, per_layer, before=0):
        return Signal(nc, name, per_layer, before)

    raw_loaded = [sig(f"raw_loaded{r}", 16 * SLOTS // RING, 16 * N_PRE // RING) for r in range(RING)]
    lo_ready = [sig(f"lo_ready{r}", SLOTS // RING, N_PRE // RING + 1) for r in range(RING)]
    late_loaded = [sig(f"late_loaded{r}", 16 * len(range(r, ADA_LATE, LATE_RING))) for r in range(LATE_RING)]
    late_used = sig("late_used", ADA_LATE)
    c_loaded = sig("c_loaded", 16)
    hi_ready = sig("hi_ready", SLOTS)
    slot_used = sig("slot_used", SLOTS, RING)
    start_loaded = sig("start_loaded", 0)
    c_exp = sig("c_exp", 1, 1)
    x_ready = sig("x_ready", 2, 1)
    tables_loaded = sig("tables_loaded", 16)
    params_loaded = sig("params_loaded", 16)
    ln_loaded = sig("ln_loaded", 64)
    mods_ready = sig("mods_ready", 2)
    xt_done = sig("xt_done", 8, 4)
    hf_done = sig("hf_done", 8)
    h_ready = sig("h_ready", 8)
    proj_out = sig("proj_out", S_PROJ)
    perm_done = sig("perm_done", 7)
    rope_done = sig("rope_done", 7)
    zpe_done = sig("zpe_done", 2)
    pads_zero = sig("pads_zero", 1)
    cmp_hid = sig("cmp_hid", 1)
    cmp_gelu = sig("cmp_gelu", 1)
    cmp_hid_turned = sig("cmp_hid_turned", 1)
    cmp_hid_out = sig("cmp_hid_out", 1)
    cmp_kv = sig("cmp_kv", 1)
    cmp_kraw = sig("cmp_kraw", 1)
    cmp_vsel = sig("cmp_vsel", 1)
    cmp_scored = sig("cmp_scored", 1)
    cmp_shift = sig("cmp_shift", 1)
    cmp_exp = sig("cmp_exp", 1)
    cmp_prob = sig("cmp_prob", 1)
    cmp_turned = sig("cmp_turned", 1)
    cmp_pt = sig("cmp_pt", 1)
    scored = sig("scored", 16)
    maxed = sig("maxed", 16)
    exped = sig("exped", 16)
    prob_ready = sig("prob_ready", 16)
    turned = sig("turned", 16)
    pt_out = sig("pt_out", 16)
    pv_done = sig("pv_done", 16)
    o_hi = sig("o_hi", 2)
    o_ready = sig("o_ready", 2)
    pooled_ready = sig("pooled_ready", POOL_G)
    pool_mixed = sig("pool_mixed", 2)
    pool_hi = sig("pool_hi", 2)
    pool_ready = sig("pool_ready", 2)
    lift_read = sig("lift_read", KT)
    merged = sig("merged", KT)
    merged_hi = sig("merged_hi", KT)
    merged_ready = sig("merged_ready", KT)
    diag_ready = sig("diag_ready", 2)
    gate_spread = sig("gate_spread", 2)
    gate_row = sig("gate_row", 2)
    var_ready = sig("var_ready", 4)
    std_ready = sig("std_ready", 4)
    shift_ready = sig("shift_ready", 4)
    normed = sig("normed", 4, 2)
    q_hi_out = sig("q_hi_out", PH)
    q_ready = sig("q_ready", PH)
    kb_zero = sig("kb_zero", 1)
    kb_hi_out = sig("kb_hi_out", 1)
    kb_lo_out = sig("kb_lo_out", 1)
    keys_scored = sig("keys_scored", PH - 1)
    scores_out = sig("scores_out", PH)
    gelu_done = sig("gelu_done", NK)
    sel_shift = sig("sel_shift", 1)
    sel_exp = sig("sel_exp", 1)
    routed = sig("routed", 1)
    sel_turned = sig("sel_turned", 1)
    sel_out = sig("sel_out", 1)
    oh2_diff = sig("oh2_diff", T // 4)
    oh2_ready = sig("oh2_ready", T // 4)
    oh1_ready = sig("oh1_ready", T // 4)
    gates_done = sig("gates_done", T // 4)
    gates_applied = sig("gates_applied", T // 4)
    g_hi_out = sig("g_hi_out", NK // 4)
    g_ready = sig("g_ready", NK // 4, 1)
    stored = sig("stored", 0)

    def mod(j):
        return mods_l[:, j * KT:(j + 1) * KT]

    def late_rows(s):
        return [i for i, at in enumerate(LATE_STEPS) if at == s]

    with nc.Block() as block:

        @block.sync
        def _(sp):
            sp.dma_start(c_silu[:], c_in.to_broadcast([P, D])).then_inc(start_loaded.sem, 16)
            sp.dma_start(kc[:], const_keep).then_inc(start_loaded.sem, 16)
            sp.dma_start(bf_stage[:], const_bf).then_inc(start_loaded.sem, 16)
            sp.dma_start(mods[:], b_ada).then_inc(start_loaded.sem, 16)
            sp.dma_start(x_sb[:], x_in.rearrange("o (a p) d -> p (o a) d", p=P)).then_inc(start_loaded.sem, 16)
            sp.dma_start(lnc[:], ln_cols).then_inc(start_loaded.sem, 16)
            with sp.Fori(0, (N_PRE + L * SLOTS) // RING + 1) as j:
                for r in range(RING):
                    sp.wait_ge(lo_ready[r].sem, j + 1)
                    sp.dma_start(raw[:, r, :], stream[RING * j + r]).then_inc(raw_loaded[r].sem, 16)
            sp.wait_ge(x_ready.sem, x_ready.at(L - 1, 2))
            sp.dma_start(out.rearrange("o (a p) d -> p (o a) d", p=P), x_sb[:]).then_inc(stored.sem, 16)
            sp.wait_ge(stored.sem, 16)

        @block.gpsimd
        def _(pool):
            def lo(l, j):
                r = RING - 1
                pool.wait_ge(hi_ready.sem, hi_ready.at(l, RING * j + RING))
                pool.tensor_tensor(w_lo[:, r, :], raw[:, r, :], w_hi[:, r, :].bitcast(F32), ALU.subtract).then_inc(lo_ready[r].sem, 1)

            def load_late(l, i):
                r = i % LATE_RING
                if i >= LATE_RING:
                    pool.wait_ge(late_used.sem, late_used.at(l, i - LATE_RING + 1))
                pool.nop()
                pool.dma_start(late_sb[:, r, :], late[l, i]).then_inc(late_loaded[r].sem, 16)

            def pooling(l, g):
                pool.wait_ge(proj_out.sem, proj_out.at(l, 12 + g))
                cur = pin[:, g, :]
                for k in range(g + 1):
                    nxt, s = psum2[:, k % 2, :], 1 << k
                    if k:
                        pool.drain()
                    pool.tensor_tensor(nxt[:, PAD:], cur[:, PAD:], cur[:, PAD - s:PAD + T - s], ALU.add)
                    cur = nxt
                pool.drain()
                pool.tensor_tensor(pooled[:, g, :], cur[:, PAD:], inv_cnt[:, g, :], ALU.mult)
                pool.drain()
                pool.tensor_tensor(pooled[:, g, :], pooled[:, g, :], pin[:, g, PAD:], ALU.subtract).then_inc(pooled_ready.sem, 1)

            def load_rows(l, which):
                for k in range(2):
                    pool.dma_start(ln_row[:, k, :], ln_gb[l, 2 * which + k].to_broadcast([P, D])).then_inc(ln_loaded.sem, 16)

            def finish(l, which):
                pool.wait_ge(ln_loaded.sem, ln_loaded.at(l, 32 * which + 32))
                pool.wait_ge(xt_done.sem, xt_done.at(l, 4 * which + 4))
                for t in range(TT):
                    pool.tensor_tensor(x_sb[:, t, :], x_sb[:, t, :], ln_row[:, 0, :], ALU.mult)
                pool.drain()
                for t in range(TT):
                    p = pool.tensor_tensor(x_sb[:, t, :], x_sb[:, t, :], ln_row[:, 1, :], ALU.add)
                p.then_inc(x_ready.sem, 1)

            pool.wait_ge(start_loaded.sem, 96)
            lo(0, 0)
            with pool.Fori(0, L) as l:
                pool.wait_ge(g_ready.sem, g_ready.at(l, 0))
                pool.tensor_tensor(pin[:, :, 0:PAD], zeros.unsqueeze(1).to_broadcast([P, POOL_G, PAD]),
                                   zeros.unsqueeze(1).to_broadcast([P, POOL_G, PAD]), ALU.mult)
                pool.memset(psum2[:, :, 0:PAD], 0.0).then_inc(pads_zero.sem, 1)
                pool.dma_start(cm[:], const_mix).then_inc(tables_loaded.sem, 16)
                pool.dma_start(wp[:], pack[l]).then_inc(params_loaded.sem, 16)
                for s in range(S_UP):
                    if s and s % RING == 0:
                        lo(l, s // RING)
                    if s == LATE_AT - 1:
                        pool.wait_ge(cmp_hid.sem, cmp_hid.at(l, 1))
                        for i in range(LATE_RING):
                            load_late(l, i)
                    for i in late_rows(s):
                        if i + LATE_RING < ADA_LATE:
                            load_late(l, i + LATE_RING)
                    if s == 13:
                        pool.wait_ge(tables_loaded.sem, tables_loaded.at(l, 16))
                    if s in (13, 14, 15, 17):
                        pooling(l, (13, 14, 15, 17).index(s))
                    if s == S_LIFT + KT + 1:
                        pool.wait_ge(merged_ready.sem, merged_ready.at(l, KT))
                        pool.nop()
                        load_rows(l, 0)
                    if s in (S_OUT + 2, S_OUT + 3, S_OUT + 4, S_OUT + 6):
                        n = (S_OUT + 2, S_OUT + 3, S_OUT + 4, S_OUT + 6).index(s)
                        z = zeros[:, 0:1].to_broadcast([P, PH * NK])
                        dst = (kb_hi if n < 2 else kb_lo)[:, (n % 2) * PH // 2:(n % 2 + 1) * PH // 2, :]
                        p = pool.tensor_tensor(dst.rearrange("p h k -> p (h k)"), z, z, ALU.mult)
                        if n == 3:
                            p.then_inc(kb_zero.sem, 1)
                    if s == S_QUERY + 1:
                        finish(l, 0)
                with pool.Fori(0, NK // RING) as i:
                    lo(l, i + S_UP // RING)
                pool.wait_ge(sel_out.sem, sel_out.at(l, 1))
                pool.wait_ge(slot_used.sem, slot_used.at(l, S_DOWN))
                pool.nop()

                def distance(k, b):
                    pool.tensor_tensor(oh2[:, b], iota.unsqueeze(1).to_broadcast([P, 4, P]),
                                       sel[:, 1, bass.ds(4 * k, 4)].unsqueeze(2).to_broadcast([P, 4, P]),
                                       ALU.subtract).then_inc(oh2_diff.sem, 1)

                for b in range(4):
                    distance(b, b)
                with pool.Fori(1, T // 16) as i:
                    for b in range(4):
                        pool.wait_ge(gates_done.sem, gates_done.at(l, 4 * i + (b - 3)))
                        pool.nop()
                        distance(4 * i + b, b)
                lo(l, S_DOWN // RING)
                pool.dma_start(c_silu[:], c_in.to_broadcast([P, D])).then_inc(c_loaded.sem, 16)
                half = (LN_END + 3) // 4
                with pool.Fori(1, half) as i:
                    lo(l, i + S_DOWN // RING)
                pool.wait_ge(g_ready.sem, g_ready.at(l, half))
                pool.nop()
                load_rows(l, 1)
                with pool.Fori(half, NK // RING + 1) as i:
                    lo(l, i + S_DOWN // RING)
                finish(l, 1)

        @block.scalar
        def _(act):
            def hi(l, j, i):
                r = i % RING
                act.wait_ge(raw_loaded[r].sem, raw_loaded[r].at(l, 16 * (j + i // RING + 1)))
                act.wait_ge(slot_used.sem, l * SLOTS + RING * j + (i + 1))
                act.activation(w_hi[:, r, :], raw[:, r, :], ACT.Copy).then_inc(hi_ready.sem, 1)

            def product(l, j, i):
                act.wait_ge(slot_used.sem, slot_used.at(l, RING * j + (i + 1)))

            def build_h(l, which, banks):
                sc, sh = mod(3 * which + 1), mod(3 * which)
                act.wait_ge(mods_ready.sem, mods_ready.at(l, which + 1))
                for k in range(KT):
                    if k % 2 == 0:
                        act.wait_ge(xt_done.sem, xt_done.at(l, 4 * which + k // 2 - 3))
                    a = act.activation(hf[:, k, :], ps[:, banks + k // 2, (k % 2) * T:(k % 2 + 1) * T], ACT.Identity,
                                       scale=sc[:, k:k + 1], bias=sh[:, k:k + 1])
                    if k % 2:
                        a.then_inc(hf_done.sem, 1)

            def norm(l, which, gate_bank):
                act.wait_ge(gate_spread.sem, gate_spread.at(l, which + 1))
                act.copy(g_row[:, 0:512], ps[:, gate_bank, :])
                act.copy(g_row[:, 512:1024], ps[:, gate_bank + 1, :]).then_inc(gate_row.sem, 1)

            def norm_end(l, which):
                for t in range(TT):
                    act.wait_ge(var_ready.sem, var_ready.at(l, 2 * which + t + 1))
                    act.activation(std[:, t:t + 1], v_eps[:, t:t + 1], ACT.Sqrt).then_inc(std_ready.sem, 1)
                    act.wait_ge(shift_ready.sem, shift_ready.at(l, 2 * which + t + 1))
                    act.activation(x_sb[:, t, :], z_ln[:, t, :], ACT.Identity, scale=rinv[:, t:t + 1],
                                   bias=nbias[:, t:t + 1]).then_inc(normed.sem, 1)

            def attend(l, n):
                if n < 16:
                    w = (n // HEADS + 1) * P
                    act.wait_ge(maxed.sem, maxed.at(l, n + 1))
                    if n >= 2:
                        act.wait_ge(turned.sem, turned.at(l, n - 1))
                    for b in range(2):
                        a = act.activation(prob[:, n % 2, b * w:(b + 1) * w], ps[:, 2 + n % 2, b * w:(b + 1) * w], ACT.Exp,
                                           bias=nmax[:, n, b:b + 1], scale=1.0, accum_out=rsum[:, n, b:b + 1])
                    a.then_inc(exped.sem, 1)
                if 1 <= n <= 16:
                    u = n - 1
                    w = 2 * (u // HEADS + 1) * P
                    act.wait_ge(turned.sem, turned.at(l, u + 1))
                    if u >= 2:
                        act.wait_ge(pv_done.sem, pv_done.at(l, u - 1))
                    act.copy(prob_t[:, u % 2, 0:w], ps[:, 4 + u % 2, 0:w]).then_inc(pt_out.sem, 1)
                if n in (10, 17):
                    t = n // 16
                    act.wait_ge(pv_done.sem, pv_done.at(l, HEADS * (t + 1)))
                    act.activation(act1_hi[:, 0:HPG, t * P:(t + 1) * P], ps[:, 6 + t, :].rearrange("p (c t) -> p c t", c=HPG),
                                   ACT.Copy).then_inc(o_hi.sem, 1)

            act.wait_ge(start_loaded.sem, 96)
            act.activation(c_tmp[:], c_silu[:], ACT.Exp, scale=-1.0).then_inc(c_exp.sem, 1)

            for i in range(RING):
                hi(0, 0, i)
            with act.Fori(0, L) as l:
                build_h(l, 0, 2)
                for s in range(S_PROJ):
                    if s:
                        hi(l, 0, s + AHEAD)
                    product(l, 0, s)
                    bank = ps[:, s % 2, 0:T]
                    if s < 8:
                        a = act.copy(qk_raw[:, s, :], bank)
                    elif s < 10:
                        a = act.copy(vtok[:, s - 8, :].rearrange("p (t c) -> p t c", t=TT),
                                     ps[:, 0, :].rearrange("p (t b c) -> p t b c", t=TT, b=2)[:, :, s - 8, :])
                    elif s == 10:
                        a = act.activation(gate3[:], bank.rearrange("p (a c) -> p a c", a=TT)[:, :, 0:24], ACT.Tanh, scale=0.5)
                    elif s < 15:
                        if s == 11:
                            act.wait_ge(pads_zero.sem, pads_zero.at(l, 1))
                        a = act.copy(pin[:, s - 11, PAD:], bank)
                    else:
                        if s == 15:
                            act.wait_ge(x_ready.sem, x_ready.at(l, 0))
                        a = act.activation(gab[:, (s - 15) % KT, (s - 15) // KT, :], bank, ACT.Tanh, scale=0.5)
                    a.then_inc(proj_out.sem, 1)
                    if s == 8:
                        act.wait_ge(cmp_hid.sem, cmp_hid.at(l, 1))
                        act.activation(hid_t[0:N_CMP].rearrange("p a c -> p (a c)"), ps[0:N_CMP, 6, 0:2 * P],
                                       ACT.Gelu_apprx_tanh).then_inc(cmp_gelu.sem, 1)
                    if s == 14:
                        act.wait_ge(cmp_shift.sem, cmp_shift.at(l, 1))
                        act.activation(pc[:], pc[:], ACT.Exp).then_inc(cmp_exp.sem, 1)
                    if s == 15:
                        act.wait_ge(cmp_turned.sem, cmp_turned.at(l, 1))
                        act.copy(pc_t[:], ps[:, 7, 0:TT * P].rearrange("p (a c) -> p a c", a=TT)).then_inc(cmp_pt.sem, 1)
                    if s >= 15:
                        attend(l, s - 15)
                for u in (16, 17):
                    attend(l, u)
                for n in range(2):
                    act.wait_ge(pool_mixed.sem, pool_mixed.at(l, n + 1))
                    for g in (2 * n, 2 * n + 1):
                        act.activation(opf[:, g, :], ps[:, 2 + n, (g % 2) * T:(g % 2 + 1) * T], ACT.Copy, scale=pool_sc[:, g:g + 1])
                    act.drain()
                    act.activation(act1_hi[:, 4 + 2 * n:6 + 2 * n, :], opf[:, 2 * n:2 * n + 2, :], ACT.Copy).then_inc(pool_hi.sem, 1)
                for k in range(KT):
                    s = S_LIFT + k
                    hi(l, 0, s + AHEAD)
                    act.wait_ge(merged.sem, merged.at(l, k + 1))
                    act.activation(act0_hi[:, k, :], mf[:, k % 2, :], ACT.Copy).then_inc(merged_hi.sem, 1)
                norm(l, 0, 6)
                for k in range(KT):
                    hi(l, 0, S_OUT + k + AHEAD)
                norm_end(l, 0)
                build_h(l, 1, 2)
                for k in range(PH):
                    hi(l, 0, S_QUERY + k + AHEAD)
                    product(l, 0, S_QUERY + k)
                    act.activation(q_hi[:, k, :], ps[:, (S_QUERY + k) % 2, 0:T], ACT.Copy).then_inc(q_hi_out.sem, 1)
                    if k == PH - 2:
                        act.drain()
                        act.wait_ge(kb_zero.sem, kb_zero.at(l, 1))
                        for p in range(2):
                            pp = slice(p * HD, (p + 1) * HD)
                            a = act.activation(kb_hi[pp, :, p * NK:(p + 1) * NK],
                                               w_hi[pp, S_KEYS % RING, :].bitcast(F32).rearrange("p (h k) -> p h k", h=PH), ACT.Copy)
                        a.then_inc(kb_hi_out.sem, 1)
                hi(l, 0, S_KEYS + AHEAD)
                act.wait_ge(x_ready.sem, x_ready.at(l, 1))
                for k in range(PH):
                    if k < PH - 1:
                        act.wait_ge(keys_scored.sem, keys_scored.at(l, k + 1))
                    else:
                        product(l, 0, S_KEYS)
                    act.copy(scores[:, 2 * k:2 * k + 2].rearrange("p u h k -> p (u h k)"),
                             ps[:, 2 + k % 4, :]).then_inc(scores_out.sem, 1)

                def up(i):
                    for n in range(RING):
                        hi(l, i + S_UP // RING, n + AHEAD)
                        product(l, i + S_UP // RING, n)
                        act.nop()
                        act.activation(experts[:, RING * i + n, :], ps[:, n % 2, 0:T], ACT.Gelu_apprx_tanh).then_inc(gelu_done.sem, 1)

                with act.Fori(0, 16) as i:
                    up(i)
                with act.Fori(16, 25) as i:
                    up(i)
                act.wait_ge(sel_shift.sem, sel_shift.at(l, 1))
                act.activation(sv[:], sv[:], ACT.Exp).then_inc(sel_exp.sem, 1)
                with act.Fori(25, ROUTE_ROW // RING) as i:
                    up(i)
                act.wait_ge(routed.sem, routed.at(l, 1))
                with act.Fori(ROUTE_ROW // RING, NK // RING - 1) as i:
                    up(i)
                act.wait_ge(sel_turned.sem, sel_turned.at(l, 1))
                act.copy(sel[:, 0:2, :].rearrange("p a t -> p (a t)"), ps[:, 2, :])
                act.copy(sel[:, 2, :], ps[:, 3, 0:T]).then_inc(sel_out.sem, 1)
                with act.Fori(NK // RING - 1, NK // RING) as i:
                    up(i)

                def one_hot(k, b):
                    act.wait_ge(oh2_diff.sem, oh2_diff.at(l, k + 1))
                    act.activation(oh2[:, b], oh2[:, b], ACT.Abs)
                    act.drain()
                    act.activation(oh2[:, b], oh2[:, b], ACT.Relu, scale=-1.0, bias=1.0).then_inc(oh2_ready.sem, 1)

                with act.Fori(0, T // 16) as i:
                    for b in range(4):
                        one_hot(4 * i + b, b)
                act.wait_ge(gates_applied.sem, gates_applied.at(l, T // 4))

                def gated(i, b):
                    act.activation(g_hi[:, b].rearrange("p a t -> p (a t)"),
                                   experts[:, bass.ds(RING * i, RING), :].rearrange("p a t -> p (a t)"), ACT.Copy).then_inc(g_hi_out.sem, 1)

                def down(i, b, more=True):
                    hi(l, i + S_DOWN // RING, AHEAD)
                    if more:
                        gated(i + 1, b)
                    for n in range(1, RING):
                        hi(l, i + S_DOWN // RING, n + AHEAD)
                    if not more:
                        hi(l, i + S_DOWN // RING, RING + AHEAD)

                gated(0, 0)
                down(0, 1)
                act.wait_ge(c_loaded.sem, c_loaded.at(l, 16))
                act.wait_ge(g_ready.sem, g_ready.at(l, 1))
                act.activation(c_tmp[:], c_silu[:], ACT.Exp, scale=-1.0).then_inc(c_exp.sem, 1)
                with act.Fori(0, 15) as h:
                    down(2 * h + 1, 0)
                    down(2 * h + 2, 1)
                norm(l, 1, 2)
                down(NK // 4 - 1, None, more=False)
                norm_end(l, 1)

        @block.vector
        def _(dve):
            def lo(l, j, i):
                r = i % RING
                if r == RING - 1:
                    return
                dve.wait_ge(hi_ready.sem, hi_ready.at(l, RING * j + (i + 1)))
                dve.tensor_tensor(w_lo[:, r, :], raw[:, r, :], w_hi[:, r, :].bitcast(F32), ALU.subtract).then_inc(lo_ready[r].sem, 1)

            def build_h(l, which, dst_hi, dst_lo):
                for n in range(KT // 2):
                    dve.wait_ge(hf_done.sem, hf_done.at(l, 4 * which + n + 1))
                    k = slice(2 * n, 2 * n + 2)
                    dve.tensor_copy(dst_hi[:, k, :], hf[:, k, :])
                    dve.drain()
                    dve.tensor_tensor(dst_lo[:, k, :], hf[:, k, :], dst_hi[:, k, :].bitcast(F32), ALU.subtract).then_inc(h_ready.sem, 1)

            def fold_norm(l, which):
                sc, sh = mod(3 * which + 1), mod(3 * which)
                gain, bias = (lnc[:, bass.ds(2 * l + which, 1), k, :].rearrange("p a k -> p (a k)") for k in range(2))
                dve.tensor_tensor(fold[:], bias, sc, ALU.mult)
                dve.drain()
                dve.tensor_tensor(sh, sh, fold[:], ALU.add)
                dve.tensor_tensor(sc, sc, gain, ALU.mult).then_inc(mods_ready.sem, 1)

            def gate_diag(l, which):
                g = mod(3 * which + 2)
                for k in range(KT):
                    d = dve.tensor_scalar(diag[:, k, :], ident, g[:, k:k + 1], None, ALU.mult)
                d.then_inc(diag_ready.sem, 1)

            def norm(l, which, bank, last_slot):
                dve.wait_ge(gate_row.sem, gate_row.at(l, which + 1))
                dve.wait_ge(x_ready.sem, x_ready.at(l, which))
                dve.wait_ge(slot_used.sem, slot_used.at(l, last_slot + 1))

                def gated_y(t):
                    for h in range(2):
                        c = slice(512 * h, 512 * h + 512)
                        dve.tensor_tensor(z_ln[:, t, c], ps[:, bank + 2 * t + h, :], g_row[:, c], ALU.mult)
                    dve.drain()

                def variance(t):
                    dve.scalar_tensor_tensor(z_ln[:, t, :], x_sb[:, t, :], ALPHA, z_ln[:, t, :], ALU.mult, ALU.add)
                    dve.drain()
                    for h in range(2):
                        dve.bn_stats(stat[:, t, h, :], z_ln[:, t, 512 * h:512 * h + 512])
                    dve.drain()
                    dve.bn_aggr(mv[:, t, :], stat[:, t].rearrange("p a b -> p (a b)"))
                    dve.drain()
                    dve.tensor_scalar(v_eps[:, t:t + 1], mv[:, t, 1:2], EPS, None, ALU.add).then_inc(var_ready.sem, 1)

                def shift(t):
                    mean, r, v, w = mv[:, t, 0:1], rinv[:, t:t + 1], v_eps[:, t:t + 1], newt[:, t:t + 1]
                    dve.wait_ge(std_ready.sem, std_ready.at(l, 2 * which + t + 1))
                    dve.reciprocal(r, std[:, t:t + 1])
                    dve.drain()
                    dve.scalar_tensor_tensor(w, v, r, r, ALU.mult, ALU.mult)
                    dve.drain()
                    dve.tensor_scalar(w, w, -0.5, 1.5, ALU.mult, ALU.add)
                    dve.drain()
                    dve.tensor_tensor(r, r, w, ALU.mult)
                    dve.drain()
                    dve.scalar_tensor_tensor(nbias[:, t:t + 1], mean, -1.0, r, ALU.mult, ALU.mult).then_inc(shift_ready.sem, 1)

                gated_y(0)
                variance(0)
                gated_y(1)
                shift(0)
                variance(1)
                shift(1)

            def rotate(l, c):
                cs = 0 if c < 4 else 2
                dve.wait_ge(perm_done.sem, perm_done.at(l, c + 1))
                dve.tensor_tensor(rope_t[:, 0, :], qk_raw[:, c, :], rope[:, cs, :], ALU.mult)
                dve.tensor_tensor(rope_t[:, 1, :], ps[:, 7, 0:T], rope[:, cs + 1, :], ALU.mult)
                dve.drain()
                dve.tensor_tensor(qk[:, c, :], rope_t[:, 0, :], rope_t[:, 1, :], ALU.add).then_inc(rope_done.sem, 1)

            def attend(l, n):
                if n < 16:
                    w = 2 * (n // HEADS + 1) * P
                    dve.wait_ge(scored.sem, scored.at(l, n + 1))
                    dve.tensor_reduce(nmax[:, n, :], ps[:, 2 + n % 2, 0:w].rearrange("p (b k) -> p b k", b=2), AX, ALU.max,
                                      negate=True).then_inc(maxed.sem, 1)
                if 1 <= n <= 16:
                    u = n - 1
                    t, h = u // HEADS, u % HEADS
                    w = (t + 1) * P
                    dve.wait_ge(exped.sem, exped.at(l, u + 1))
                    dve.reciprocal(rsum[:, u, :], rsum[:, u, :])
                    dve.drain()
                    dve.tensor_tensor(rsum[:, u, :], rsum[:, u, :], gate3[:, t, 3 * h + 1:3 * h + 3], ALU.mult)
                    dve.drain()
                    for b in range(2):
                        d = dve.tensor_scalar(prob[:, u % 2, b * w:(b + 1) * w], prob[:, u % 2, b * w:(b + 1) * w],
                                              rsum[:, u, b:b + 1], None, ALU.mult)
                    d.then_inc(prob_ready.sem, 1)
                if n in (10, 17):
                    t = n // 16
                    dve.wait_ge(o_hi.sem, o_hi.at(l, t + 1))
                    tc = slice(t * P, (t + 1) * P)
                    dve.tensor_tensor(act1_lo[:, 0:HPG, tc], ps[:, 6 + t, :].rearrange("p (c t) -> p c t", c=HPG),
                                      act1_hi[:, 0:HPG, tc].bitcast(F32), ALU.subtract).then_inc(o_ready.sem, 1)

            def silu(l):
                dve.wait_ge(c_exp.sem, c_exp.at(l, 1))
                dve.tensor_scalar(c_tmp[:], c_tmp[:], 1.0, None, ALU.add)
                dve.drain()
                dve.reciprocal(c_tmp[:], c_tmp[:])
                dve.drain()
                dve.tensor_tensor(c_silu[:], c_silu[:], c_tmp[:], ALU.mult)
                dve.drain()

            def late_row(l, i):
                r = i % LATE_RING
                row = late_sb[:, r, :]
                dve.wait_ge(late_loaded[r].sem, late_loaded[r].at(l, 16 * (i // LATE_RING + 1)))
                dve.tensor_tensor_reduce(row, row, c_silu[:], 1.0, 0.0, ALU.mult, ALU.add,
                                         acc_late[:, i:i + 1]).then_inc(late_used.sem, 1)

            def add_bias(j0, j1):
                dve.drain()
                dve.tensor_tensor(mods_l[:, j0 * KT:j1 * KT], mods_l[:, j0 * KT:j1 * KT],
                                  acc_late[:, j0 * KT - ADA_PRE:j1 * KT - ADA_PRE], ALU.add)
                dve.drain()

            dve.drain().then_inc(lo_ready[0].sem, 1)
            dve.drain().then_inc(lo_ready[1].sem, 1)
            dve.drain().then_inc(lo_ready[2].sem, 1)
            dve.drain().then_inc(lo_ready[3].sem, 1)
            dve.drain().then_inc(g_ready.sem, 1)
            dve.wait_ge(start_loaded.sem, 96)
            dve.tensor_copy(bfc[:], bf_stage[:]).then_inc(x_ready.sem, 1)
            dve.drain().then_inc(normed.sem, TT)
            silu(-1)
            for l in range(L):
                with dve.Fori(0, ADA_PRE // RING) as j:
                    for r in range(RING):
                        dve.wait_ge(raw_loaded[r].sem, 16 * j + 16 * (1 + l * ADA_PRE // RING))
                        dve.tensor_tensor_reduce(raw[:, r, :], raw[:, r, :], c_silu[:], 1.0, 0.0, ALU.mult, ALU.add,
                                                 acc4[:, r:r + 1]).then_inc(lo_ready[r].sem, 1)
                    dve.drain()
                    dve.tensor_tensor(mods[:, bass.ds(RING * j + l * ADA, RING)], mods[:, bass.ds(RING * j + l * ADA, RING)],
                                      acc4[:], ALU.add)
                    dve.drain()
                sc = mods[:, l * ADA + KT:l * ADA + 2 * KT]
                dve.tensor_scalar(sc, sc, 1.0, None, ALU.add)
            dve.drain()

            for i in range(AHEAD):
                lo(0, 0, i)
            with dve.Fori(0, L) as l:
                dve.tensor_copy(mods_l[:], mods[:, bass.ds(l * ADA, ADA)])
                dve.drain()
                fold_norm(l, 0)
                build_h(l, 0, act0_hi, act0_lo)
                for s in range(S_PROJ):
                    lo(l, 0, s + AHEAD)
                    if s == 2:
                        dve.wait_ge(tables_loaded.sem, tables_loaded.at(l, 16))
                    if s == 2:
                        dve.memset(hid_t[:], 0.0)
                    for i in late_rows(s):
                        late_row(l, i)
                    if 2 <= s <= 7:
                        rotate(l, s - 2)
                    if s == 8:
                        dve.wait_ge(params_loaded.sem, params_loaded.at(l, 16))
                        for a in range(2):
                            dve.wait_ge(proj_out.sem, proj_out.at(l, 7 + a))
                            for h in range(2):
                                d = dve.tensor_tensor(zpe[:, a, h, :].rearrange("p (n c) -> p n c", c=CMP_STRIDE),
                                                      qk_raw[:, 6 + a, :].rearrange("p (n c) -> p n c", c=CMP_STRIDE),
                                                      cmp_pe[:, a, h * CMP_STRIDE:(h + 1) * CMP_STRIDE].unsqueeze(1)
                                                      .to_broadcast([P, T // CMP_STRIDE, CMP_STRIDE]), ALU.add)
                            d.then_inc(zpe_done.sem, 1)
                    if s == 10:
                        dve.wait_ge(cmp_hid_turned.sem, cmp_hid_turned.at(l, 1))
                        dve.tensor_copy(hid_k[:], ps[:, 6, 2 * P:2 * P + CP])
                        dve.tensor_copy(hid_v[:], ps[:, 6, 3 * P:3 * P + CP].unsqueeze(1)
                                        .to_broadcast([P, HEADS, CP])).then_inc(cmp_hid_out.sem, 1)
                    if s == 11:
                        dve.wait_ge(proj_out.sem, proj_out.at(l, 11))
                        dve.tensor_scalar(gate3[:], gate3[:], 0.5, 0.5, ALU.mult, ALU.add)
                        dve.wait_ge(cmp_kv.sem, cmp_kv.at(l, 1))
                        dve.tensor_copy(kc_raw[:], ps[:, 6, 2 * CP:3 * CP]).then_inc(cmp_kraw.sem, 1)
                        dve.tensor_tensor(vc_sel[:], ps[:, 6, P:2 * P].unsqueeze(1).to_broadcast([P, HPG, P]), vsel, ALU.mult).then_inc(cmp_vsel.sem, 1)
                    if s == 12:
                        dve.wait_ge(perm_done.sem, perm_done.at(l, 7))
                        dve.tensor_tensor(kc_t1[:], kc_raw[:], crope[:, 0, :], ALU.mult)
                        dve.tensor_tensor(kc_rot[:], ps[:, 7, 0:CP], crope[:, 1, :], ALU.mult)
                        dve.drain()
                        dve.tensor_tensor(kc_rot[:], kc_rot[:], kc_t1[:], ALU.add).then_inc(rope_done.sem, 1)
                    if s == 14:
                        dve.wait_ge(cmp_scored.sem, cmp_scored.at(l, 1))
                        for t in range(TT):
                            for g in range(GROUPS):
                                sc = ps[:, 6 + g, T + t * HPG * CP:T + (t + 1) * HPG * CP].rearrange("p (h c) -> p h c", c=CP)
                                dve.tensor_tensor(pc[:, t, g * HPG:(g + 1) * HPG], sc, cmask[:, t, :].unsqueeze(1).to_broadcast([P, HPG, CP]), ALU.add)
                        dve.drain()
                        dve.tensor_reduce(pc_m[:].rearrange("p a h -> p (a h)"), pc[:].rearrange("p a h c -> p (a h) c"), AX, ALU.max)
                        dve.drain()
                        dve.tensor_tensor(pc[:].rearrange("p a h c -> p (a h) c"), pc[:].rearrange("p a h c -> p (a h) c"),
                                          pc_m[:].rearrange("p a h -> p (a h)").unsqueeze(2).to_broadcast([P, TT * HEADS, CP]),
                                          ALU.subtract).then_inc(cmp_shift.sem, 1)
                    if s == 15:
                        dve.wait_ge(cmp_exp.sem, cmp_exp.at(l, 1))
                        dve.tensor_reduce(pc_m[:].rearrange("p a h -> p (a h)"), pc[:].rearrange("p a h c -> p (a h) c"), AX, ALU.add)
                        dve.drain()
                        dve.reciprocal(pc_m[:], pc_m[:])
                        dve.drain()
                        for t in range(TT):
                            dve.scalar_tensor_tensor(pc_m[:, t, :], pc_m[:, t, :], any_vis[:, t:t + 1],
                                                     gate3[:, t, :].rearrange("p (h b) -> p b h", b=3)[:, 0, :], ALU.mult, ALU.mult)
                        dve.drain()
                        dve.tensor_tensor(pc[:].rearrange("p a h c -> p (a h) c"), pc[:].rearrange("p a h c -> p (a h) c"),
                                          pc_m[:].rearrange("p a h -> p (a h)").unsqueeze(2).to_broadcast([P, TT * HEADS, CP]),
                                          ALU.mult).then_inc(cmp_prob.sem, 1)
                    if s >= 15:
                        attend(l, s - 15)
                attend(l, 16)
                attend(l, 17)
                for n in range(2):
                    dve.wait_ge(pool_hi.sem, pool_hi.at(l, n + 1))
                    dve.tensor_tensor(act1_lo[:, 4 + 2 * n:6 + 2 * n, :], opf[:, 2 * n:2 * n + 2, :],
                                      act1_hi[:, 4 + 2 * n:6 + 2 * n, :].bitcast(F32), ALU.subtract).then_inc(pool_ready.sem, 1)
                def merge_lo(k):
                    dve.wait_ge(merged_hi.sem, merged_hi.at(l, k + 1))
                    dve.tensor_tensor(act0_lo[:, k, :], mf[:, k % 2, :], act0_hi[:, k, :].bitcast(F32), ALU.subtract).then_inc(merged_ready.sem, 1)

                for k in range(KT):
                    s = S_LIFT + k
                    lo(l, 0, s + AHEAD)
                    dve.wait_ge(slot_used.sem, slot_used.at(l, s + 1))
                    dve.scalar_tensor_tensor(prod[:, k % 2], gab[:, k], 1.0, ps[:, k % 2, :].rearrange("p (a t) -> p a t", a=2),
                                             ALU.add, ALU.mult).then_inc(lift_read.sem, 1)
                    dve.drain()
                    dve.tensor_tensor(mf[:, k % 2, :], prod[:, k % 2, 0, :], prod[:, k % 2, 1, :], ALU.add).then_inc(merged.sem, 1)
                    if k:
                        merge_lo(k - 1)
                merge_lo(KT - 1)
                add_bias(2, 5)
                dve.tensor_scalar(mod(2), mod(2), 0.5, None, ALU.mult)
                dve.tensor_scalar(mod(4), mod(4), 1.0, None, ALU.add)
                dve.drain()
                gate_diag(l, 0)
                fold_norm(l, 1)
                for k in range(KT):
                    lo(l, 0, S_OUT + k + AHEAD)
                norm(l, 0, 2, S_OUT + KT - 1)
                build_h(l, 1, act1_hi, act1_lo)
                for k in range(PH):
                    lo(l, 0, S_QUERY + k + AHEAD)
                    late_row(l, 3 * KT + k)
                    dve.wait_ge(q_hi_out.sem, q_hi_out.at(l, k + 1))
                    dve.tensor_tensor(q_lo[:, k, :], ps[:, (S_QUERY + k) % 2, 0:T], q_hi[:, k, :].bitcast(F32), ALU.subtract).then_inc(q_ready.sem, 1)
                    if k == PH - 2:
                        dve.wait_ge(kb_zero.sem, kb_zero.at(l, 1))
                        dve.wait_ge(lo_ready[S_KEYS % RING].sem, lo_ready[S_KEYS % RING].at(l, S_KEYS // RING + 1))
                        for p in range(2):
                            pp = slice(p * HD, (p + 1) * HD)
                            d = dve.tensor_copy(kb_lo[pp, :, p * NK:(p + 1) * NK],
                                                w_lo[pp, S_KEYS % RING, :].bitcast(F32).rearrange("p (h k) -> p h k", h=PH))
                        d.then_inc(kb_lo_out.sem, 1)
                add_bias(5, 6)
                dve.wait_ge(scores_out.sem, scores_out.at(l, PH))
                lo(l, 0, S_KEYS + AHEAD)

                def best16(vals, idx, src, rest, between):
                    n = len(src)
                    for p in range(n):
                        dve.max(vals[p][:, 0:8], src[p])
                    dve.drain()
                    for p in range(n):
                        dve.match_replace(rest[p], vals[p][:, 0:8], src[p], -3e38)
                        dve.max_index(idx[p][:, 0:8], vals[p][:, 0:8], src[p])
                    between()
                    dve.drain()
                    for p in range(n):
                        dve.max(vals[p][:, 8:16], rest[p])
                    dve.drain()
                    for p in range(n):
                        dve.max_index(idx[p][:, 8:16], vals[p][:, 8:16], rest[p])

                with dve.Fori(0, 16) as i:
                    j = i + S_UP // RING
                    lo(l, j, AHEAD)
                    dve.tensor_copy(work_s[:], scores[:, bass.ds(i, 1)].rearrange("p u h k -> p (u h) k"))
                    dve.drain()
                    best16([half_v[:, 0, :], half_v[:, 1, :]], [ij_s[:, 0, :], ij_s[:, 1, :]],
                           [work_s[:, 0, :], work_s[:, 1, :]], [work[:, 0, :], work[:, 1, :]],
                           lambda: lo(l, j, AHEAD + 1))
                    dve.tensor_tensor(cand[:], half_v[:, 0, :].unsqueeze(2).to_broadcast([P, TOPK, TOPK]),
                                      half_v[:, 1, :].unsqueeze(1).to_broadcast([P, TOPK, TOPK]), ALU.add)
                    lo(l, j, AHEAD + 2)
                    dve.drain()
                    best16([sv_s[:]], [ci_s[:]], [cand[:].rearrange("p a b -> p (a b)")],
                           [cand2[:].rearrange("p a b -> p (a b)")], lambda: lo(l, j, AHEAD + 3))
                    dve.drain()
                    dve.tensor_copy(sv[:, bass.ds(i, 1), :], sv_s[:].unsqueeze(1))
                    dve.tensor_copy(ci[:, bass.ds(i, 1), :], ci_s[:].unsqueeze(1))
                    dve.tensor_copy(ij[:, bass.ds(i, 1)], ij_s[:].unsqueeze(1))
                    dve.drain()

                with dve.Fori(16, 24) as i:
                    j = i + S_UP // RING
                    for w in range(2):
                        u = 2 * i + (w - 32)
                        lo(l, j, AHEAD + 2 * w)
                        dve.tensor_scalar(ab[:, 0, :], ci[:, bass.ds(u, 1), :].rearrange("p a k -> p (a k)"), 4, None, ALU.logical_shift_right)
                        dve.tensor_scalar(ab[:, 1, :], ci[:, bass.ds(u, 1), :].rearrange("p a k -> p (a k)"), TOPK - 1, None, ALU.bitwise_and)
                        dve.tensor_copy(ij_f[:], ij[:, bass.ds(u, 1)].rearrange("p a h k -> p (a h) k"))
                        dve.drain()
                        for h in range(2):
                            dve.tensor_tensor(onehot[:, h], ab[:, h, :].unsqueeze(2).to_broadcast([P, TOPK, TOPK]),
                                              iota[:, 0:TOPK].unsqueeze(1).to_broadcast([P, TOPK, TOPK]), ALU.is_equal)
                        lo(l, j, AHEAD + 2 * w + 1)
                        dve.drain()
                        for h in range(2):
                            dve.tensor_tensor(onehot[:, h], onehot[:, h], ij_f[:, h, :].unsqueeze(1).to_broadcast([P, TOPK, TOPK]), ALU.mult)
                        dve.drain()
                        for h in range(2):
                            dve.tensor_reduce(sel[:, h, bass.ds(TOPK * u, TOPK)], onehot[:, h], AX, ALU.add)
                dve.drain()
                dve.tensor_copy(rsm[:], sv[:, :, 0])
                dve.drain()
                dve.tensor_tensor(sv[:], sv[:], rsm[:].unsqueeze(2).to_broadcast([P, 2 * PH, TOPK]), ALU.subtract).then_inc(sel_shift.sem, 1)
                with dve.Fori(24, 26) as i:
                    for n in range(RING):
                        lo(l, i + S_UP // RING, n + AHEAD)
                dve.wait_ge(sel_exp.sem, sel_exp.at(l, 1))
                dve.tensor_reduce(rsm[:], sv[:], AX, ALU.add)
                dve.drain()
                dve.reciprocal(rsm[:], rsm[:])
                dve.drain()
                dve.tensor_tensor(sel[:, 2, :].rearrange("p (u k) -> p u k", k=TOPK), sv[:],
                                  rsm[:].unsqueeze(2).to_broadcast([P, 2 * PH, TOPK]), ALU.mult).then_inc(routed.sem, 1)
                with dve.Fori(26, NK // RING) as i:
                    for n in range(RING):
                        lo(l, i + S_UP // RING, n + AHEAD)
                dve.wait_ge(sel_out.sem, sel_out.at(l, 1))
                dve.wait_ge(slot_used.sem, slot_used.at(l, S_DOWN))

                def weighted(k, b):
                    for t in range(4):
                        tok = 4 * k + t
                        d = dve.tensor_scalar(oh1g[:, b, t, :], iota, sel[:, 0, bass.ds(tok, 1)], sel[:, 2, bass.ds(tok, 1)],
                                              ALU.is_equal, ALU.mult)
                    d.then_inc(oh1_ready.sem, 1)

                def apply_gates(k, b):
                    dve.wait_ge(gates_done.sem, gates_done.at(l, k + 1))
                    e = experts[:, :, bass.ds(4 * k, 4)].rearrange("p i t -> p t i")
                    dve.tensor_tensor(e, e, ps[:, 2 + b, :].rearrange("p (t i) -> p t i", t=4), ALU.mult).then_inc(gates_applied.sem, 1)

                for b in range(2):
                    weighted(b, b)
                with dve.Fori(0, T // 8 - 1) as i:
                    for b in range(2):
                        apply_gates(2 * i + b, b)
                        weighted(2 * i + (b + 2), b)
                for b in range(2):
                    apply_gates(T // 4 - 2 + b, b)

                def gated(i, b):
                    dve.wait_ge(g_hi_out.sem, g_hi_out.at(l, i + 1))
                    dve.tensor_tensor(g_lo[:, b].rearrange("p a t -> p (a t)"), experts[:, bass.ds(RING * i, RING), :].rearrange("p a t -> p (a t)"),
                                      g_hi[:, b].rearrange("p a t -> p (a t)").bitcast(F32), ALU.subtract).then_inc(g_ready.sem, 1)

                def down(i, b, more=True):
                    if more:
                        gated(i + 1, b)
                    for n in range(1, RING):
                        lo(l, i + S_DOWN // RING, n + AHEAD)

                gated(0, 0)
                down(0, 1)
                silu(l)
                with dve.Fori(0, 15) as h:
                    down(2 * h + 1, 0)
                    down(2 * h + 2, 1)
                gate_diag(l, 1)
                down(NK // 4 - 1, None, more=False)
                norm(l, 1, 4, SLOTS - 1)

        @block.tensor
        def _(pe):
            mm = pe.matmul

            def split_ready(l, j, i):
                r = i % RING
                pe.wait_ge(lo_ready[r].sem, lo_ready[r].at(l, j + (i // RING + 1)))

            def turn_x(l, which, banks):
                for t in range(TT):
                    pe.wait_ge(normed.sem, normed.at(l, 2 * which + t - 1))
                    for k in range(KT):
                        m = pe.transpose(ps[:, banks + k // 2, (k % 2) * T + t * P:(k % 2) * T + (t + 1) * P],
                                         x_sb[:, t, k * P:(k + 1) * P], ident)
                        if t == TT - 1 and k % 2:
                            m.then_inc(xt_done.sem, 1)

            def by_features(dst, r, a_hi, a_lo, kts, w_at=0, ready=None):
                n = len(kts)
                for q, k in enumerate(kts):
                    if ready is not None and k % 2 == 0:
                        pe.wait_ge(h_ready.sem, ready + k // 2 + 1)
                    wc = slice((w_at + q) * P, (w_at + q + 1) * P)
                    mm(dst, w_hi[:, r, wc], a_hi[:, k, :], start=(q == 0), stop=False)
                    mm(dst, w_hi[:, r, wc], a_lo[:, k, :], start=False, stop=False)
                    m = mm(dst, w_lo[:, r, wc], a_hi[:, k, :], start=False, stop=(q == n - 1))
                return m

            def by_tokens(dst, w):
                for t in range(TT):
                    tc = slice(t * P, (t + 1) * P)
                    for k in range(KT):
                        mm(dst(t), act0_hi[:, k, tc], w(w_hi, k), start=(k == 0), stop=False)
                        mm(dst(t), act0_hi[:, k, tc], w(w_lo, k), start=False, stop=False)
                        m = mm(dst(t), act0_lo[:, k, tc], w(w_hi, k), start=False, stop=(k == KT - 1))
                return m

            def spread_gate(l, which, bank):
                pe.wait_ge(diag_ready.sem, diag_ready.at(l, which + 1))
                for k in range(KT):
                    m = mm(ps[:, bank + k // 4, (k % 4) * P:(k % 4 + 1) * P], ones, diag[:, k, :], start=True, stop=True)
                m.then_inc(gate_spread.sem, 1)

            def head(u):
                t, h = u // HEADS, u % HEADS
                return t, h % HPG, h // HPG, (h // HPG) * HD

            def score(l, u):
                t, c, g, p0 = head(u)
                n = (t + 1) * P
                if u >= 2:
                    pe.wait_ge(exped.sem, exped.at(l, u - 1))
                for b in range(2):
                    dst = ps[:, 2 + u % 2, b * n:(b + 1) * n]
                    mm(dst, qk[p0:p0 + HD, c, t * P:(t + 1) * P], qk[p0:p0 + HD, 4 + b, 0:n], start=True, stop=False)
                    m = mm(ps[:, 2 + u % 2, b * n + t * P:(b + 1) * n], ident_bf, mask_bf, start=False, stop=True)
                m.then_inc(scored.sem, 1)

            def turn_prob(l, u):
                t = u // HEADS
                pe.wait_ge(prob_ready.sem, prob_ready.at(l, u + 1))
                if u >= 2:
                    pe.wait_ge(pt_out.sem, pt_out.at(l, u - 1))
                for k in range(2 * (t + 1)):
                    m = pe.transpose(ps[:, 4 + u % 2, k * P:(k + 1) * P], prob[:, u % 2, k * P:(k + 1) * P], ident)
                m.then_inc(turned.sem, 1)

            def mix_values(l, u):
                t, c, g, p0 = head(u)
                bank = 6 + t
                if u % HEADS == 0:
                    pe.wait_ge(cmp_pt.sem, cmp_pt.at(l, 1))
                    pe.wait_ge(cmp_vsel.sem, cmp_vsel.at(l, 1))
                    for k in range(HPG):
                        mm(ps[:, bank, k * P:(k + 1) * P], vc_sel[:, k, :], pc_t[:, t, :], start=(k == 0), stop=False, skip_group_check=True)
                pe.wait_ge(pt_out.sem, pt_out.at(l, u + 1))
                for b in range(2):
                    for k in range(t + 1):
                        m = mm(ps[p0:p0 + HD, bank, c * P:(c + 1) * P], vtok[:, b, k * P + g * HD:k * P + (g + 1) * HD],
                               prob_t[:, u % 2, (b * (t + 1) + k) * P:(b * (t + 1) + k + 1) * P], start=False,
                               stop=(u % HEADS == HEADS - 1 and b == 1 and k == t), skip_group_check=True)
                m.then_inc(pv_done.sem, 1)

            pe.drain().then_inc(slot_used.sem, RING)
            pe.wait_ge(start_loaded.sem, 96)
            turn_x(0, 0, 2)
            with pe.Fori(0, L) as l:
                for s in range(S_PROJ):
                    if s >= 15:
                        if s == 15:
                            pe.wait_ge(rope_done.sem, rope_done.at(l, 7))
                        score(l, s - 15)
                    split_ready(l, 0, s)
                    if s >= 2:
                        pe.wait_ge(proj_out.sem, proj_out.at(l, s if s == 10 else s - 1))
                    if s == 8:
                        split_ready(l, 0, 9)
                        v = 8 % RING
                        m = by_tokens(lambda t: ps[:, 0, t * 2 * P:(t + 1) * 2 * P].rearrange("p (b c) -> p b c", b=2),
                                      lambda w, k: w[:, v:v + 2, k * P:(k + 1) * P])
                    elif s == 10:
                        m = by_tokens(lambda t: ps[:, 0, t * P:t * P + 3 * HEADS],
                                      lambda w, k: w[:, 10 % RING, k * P:k * P + 3 * HEADS])
                    elif s != 9:
                        m = by_features(ps[:, s % 2, 0:T], s % RING, act0_hi, act0_lo, range(KT),
                                        ready=h_ready.at(l, 0) if s == 0 else None)
                    if s != 9:
                        m.then_inc(slot_used.sem, 2 if s == 8 else 1)
                    if 1 <= s <= 6:
                        c = s - 1
                        pe.wait_ge(proj_out.sem, proj_out.at(l, c + 1))
                        if c:
                            pe.wait_ge(rope_done.sem, rope_done.at(l, c))
                        mm(ps[:, 7, 0:T], perm, qk_raw[:, c, :], start=True, stop=True).then_inc(perm_done.sem, 1)
                    if s == 8:
                        for a in range(2):
                            pe.wait_ge(zpe_done.sem, zpe_done.at(l, a + 1))
                            for n in range(CMP_LEN):
                                src = zpe[:, a, n // CMP_STRIDE, :].rearrange("p (n c) -> p c n", c=CMP_STRIDE)
                                n0 = n // CMP_STRIDE
                                m = mm(ps[0:N_CMP, 6, a * P:(a + 1) * P], src[:, n % CMP_STRIDE, n0:n0 + N_CMP], cmp_w1[:, a, n, :],
                                       start=(n == 0), stop=(n == CMP_LEN - 1))
                        m.then_inc(cmp_hid.sem, 1)
                    if s == 9:
                        pe.wait_ge(cmp_gelu.sem, cmp_gelu.at(l, 1))
                        for a in range(2):
                            m = pe.transpose(ps[:, 6, (2 + a) * P:(3 + a) * P], hid_t[:, a, :], ident)
                        m.then_inc(cmp_hid_turned.sem, 1)
                    if s == 10:
                        pe.wait_ge(cmp_hid_out.sem, cmp_hid_out.at(l, 1))
                        mm(ps[:, 6, 2 * CP:3 * CP], cmp_w2[:, 0, :], hid_k[:], start=True, stop=True)
                        mm(ps[:, 6, P:2 * P], hid_v[:].rearrange("p h c -> p (h c)"), cmp_w2[:, 1, :], start=True, stop=True).then_inc(cmp_kv.sem, 1)
                    if s == 11:
                        pe.wait_ge(cmp_kraw.sem, cmp_kraw.at(l, 1))
                        pe.wait_ge(rope_done.sem, rope_done.at(l, 6))
                        mm(ps[:, 7, 0:CP], perm, kc_raw[:], start=True, stop=True).then_inc(perm_done.sem, 1)
                    if s == 13:
                        pe.wait_ge(rope_done.sem, rope_done.at(l, 7))
                        pe.wait_ge(cmp_vsel.sem, cmp_vsel.at(l, 1))
                        for u in range(2 * HEADS):
                            t, c, g, p0 = head(u)
                            at = T + (t * HPG + c) * CP
                            m = mm(ps[:, 6 + g, at:at + CP], qk[p0:p0 + HD, c, t * P:(t + 1) * P], kc_rot[p0:p0 + HD, :], start=True, stop=True)
                        m.then_inc(cmp_scored.sem, 1)
                    if s == 15:
                        pe.wait_ge(cmp_prob.sem, cmp_prob.at(l, 1))
                        for t in range(TT):
                            m = pe.transpose(ps[:, 7, t * P:(t + 1) * P], pc[:, t].rearrange("p h c -> p (h c)"), ident)
                        m.then_inc(cmp_turned.sem, 1)
                    if s >= 16:
                        turn_prob(l, s - 16)
                    if s >= 17:
                        mix_values(l, s - 17)
                turn_prob(l, 15)
                mix_values(l, 14)
                mix_values(l, 15)
                for n in range(2):
                    pe.wait_ge(exped.sem, exped.at(l, 15 + n))
                    pe.wait_ge(pooled_ready.sem, pooled_ready.at(l, 2 * n + 2))
                    for g in (2 * n, 2 * n + 1):
                        m = mm(ps[:, 2 + n, (g % 2) * T:(g % 2 + 1) * T], w_pool[:, g, :], pooled[:, g, :], start=True, stop=True)
                    m.then_inc(pool_mixed.sem, 1)
                pe.wait_ge(o_ready.sem, o_ready.at(l, 2))
                pe.wait_ge(pool_ready.sem, pool_ready.at(l, 2))
                for k in range(KT):
                    s = S_LIFT + k
                    split_ready(l, 0, s)
                    if k < 2:
                        pe.wait_ge(proj_out.sem, proj_out.at(l, S_PROJ))
                    else:
                        pe.wait_ge(lift_read.sem, lift_read.at(l, k - 1))
                    by_features(ps[:, k % 2, 0:T], s % RING, act1_hi, act1_lo, range(0, 4))
                    by_features(ps[:, k % 2, T:2 * T], s % RING, act1_hi, act1_lo, range(4, 8), w_at=4).then_inc(slot_used.sem, 1)
                spread_gate(l, 0, 6)
                for k in range(KT):
                    s = S_OUT + k
                    split_ready(l, 0, s)
                    pe.wait_ge(merged_ready.sem, merged_ready.at(l, k + 1))
                    for t in range(TT):
                        tc = slice(t * P, (t + 1) * P)
                        for h in range(2):
                            wc = slice(512 * h, 512 * h + 512)
                            dst = ps[:, 2 + 2 * t + h, :]
                            mm(dst, act0_hi[:, k, tc], w_hi[:, s % RING, wc], start=(k == 0), stop=False)
                            mm(dst, act0_hi[:, k, tc], w_lo[:, s % RING, wc], start=False, stop=False)
                            m = mm(dst, act0_lo[:, k, tc], w_hi[:, s % RING, wc], start=False, stop=(k == KT - 1))
                    m.then_inc(slot_used.sem, 1)
                turn_x(l, 1, 2)
                for k in range(PH):
                    s = S_QUERY + k
                    split_ready(l, 0, s)
                    if k >= 2:
                        pe.wait_ge(q_ready.sem, q_ready.at(l, k - 1))
                    by_features(ps[:, s % 2, 0:T], s % RING, act1_hi, act1_lo, range(KT),
                                ready=h_ready.at(l, 4) if k == 0 else None).then_inc(slot_used.sem, 1)
                pe.wait_ge(q_ready.sem, q_ready.at(l, PH))
                pe.wait_ge(kb_hi_out.sem, kb_hi_out.at(l, 1))
                pe.wait_ge(kb_lo_out.sem, kb_lo_out.at(l, 1))
                for k in range(PH):
                    if k >= 4:
                        pe.wait_ge(scores_out.sem, scores_out.at(l, k - 3))
                    for v in range(2):
                        t, h = (2 * k + v) // PH, (2 * k + v) % PH
                        tc = slice(t * P, (t + 1) * P)
                        dst = ps[:, 2 + k % 4, v * 2 * NK:(v + 1) * 2 * NK]
                        mm(dst, q_hi[:, h, tc], kb_hi[:, h, :], start=True, stop=False)
                        mm(dst, q_hi[:, h, tc], kb_lo[:, h, :], start=False, stop=False)
                        m = mm(dst, q_lo[:, h, tc], kb_hi[:, h, :], start=False, stop=True)
                    m.then_inc(keys_scored.sem if k < PH - 1 else slot_used.sem, 1)

                def up(i, first):
                    for n in range(RING):
                        split_ready(l, i + S_UP // RING, n)
                        if not (first and n < 2):
                            pe.wait_ge(gelu_done.sem, gelu_done.at(l, RING * i + (n - 1)))
                        by_features(ps[:, n % 2, 0:T], n, act1_hi, act1_lo, range(KT)).then_inc(slot_used.sem, 1)

                up(0, True)
                with pe.Fori(1, NK // RING - 1) as i:
                    up(i, False)
                pe.wait_ge(routed.sem, routed.at(l, 1))
                for a in range(3):
                    for t in range(TT):
                        at = a * T + t * P
                        m = pe.transpose(ps[:, 2 + at // 512, at % 512:at % 512 + P], sel[:, a, t * P:(t + 1) * P], ident)
                m.then_inc(sel_turned.sem, 1)
                with pe.Fori(NK // RING - 1, NK // RING) as i:
                    up(i, False)

                def gates(k, b, first):
                    pe.wait_ge(oh2_ready.sem, oh2_ready.at(l, k + 1))
                    pe.wait_ge(oh1_ready.sem, oh1_ready.at(l, k + 1))
                    if first:
                        pe.wait_ge(sel_out.sem, sel_out.at(l, 1))
                    else:
                        pe.wait_ge(gates_applied.sem, gates_applied.at(l, k - 1))
                    for t in range(4):
                        m = mm(ps[:, 2 + b % 2, t * P:(t + 1) * P], oh2[:, b, t, :], oh1g[:, b % 2, t, :], start=True, stop=True)
                    m.then_inc(gates_done.sem, 1)

                for b in range(4):
                    gates(b, b, b < 2)
                with pe.Fori(1, T // 16) as i:
                    for b in range(4):
                        gates(4 * i + b, b, False)

                def down(i, b, first=False, last=False):
                    pe.wait_ge(g_ready.sem, g_ready.at(l, i + 1))
                    for n in range(RING):
                        split_ready(l, i + S_DOWN // RING, n)
                        for t in range(TT):
                            tc = slice(t * P, (t + 1) * P)
                            for h in range(2):
                                wc = slice(512 * h, 512 * h + 512)
                                dst = ps[:, 4 + 2 * t + h, :]
                                mm(dst, g_hi[:, b, n, tc], w_hi[:, n, wc], start=(first and n == 0), stop=False, skip_group_check=True)
                                mm(dst, g_hi[:, b, n, tc], w_lo[:, n, wc], start=False, stop=False, skip_group_check=True)
                                m = mm(dst, g_lo[:, b, n, tc], w_hi[:, n, wc], start=False, stop=(last and n == RING - 1), skip_group_check=True)
                        m.then_inc(slot_used.sem, 1)

                down(0, 0, first=True)
                with pe.Fori(0, 15) as h:
                    down(2 * h + 1, 1)
                    down(2 * h + 2, 0)
                spread_gate(l, 1, 2)
                down(NK // 4 - 1, 1, last=True)
                turn_x(l, 2, 2)


def _tables():
    f = np.float32
    keep = np.zeros((P, KEEP), f)
    keep[:, K_IDENT:K_IDENT + P] = np.eye(P, dtype=f)
    half = ROT // 2
    for g in range(GROUPS):
        for i in range(half):
            keep[g * HD + i, K_PERM + g * HD + i + half] = 1
            keep[g * HD + i + half, K_PERM + g * HD + i] = 1
    keep[:, K_IOTA:K_IOTA + P] = np.arange(P, dtype=f)
    keep[:, K_ONES:K_ONES + P] = 1

    def rot(pos):
        inv = f(500000.0) ** (-np.arange(0, ROT, 2, dtype=f) / f(ROT))
        ang = pos.astype(f)[:, None] * inv[None, :].astype(f)
        c, s = np.ones((P, len(pos)), f), np.zeros((P, len(pos)), f)
        for g in range(GROUPS):
            for i in range(half):
                a, b = g * HD + i, g * HD + i + half
                c[a] = c[b] = np.cos(ang[:, i])
                s[a], s[b] = -np.sin(ang[:, i]), np.sin(ang[:, i])
        return c, s

    mix = np.zeros((P, MIX), f)
    c, s = rot(np.arange(T))
    mix[:, M_ROPE:M_CROPE] = np.concatenate([c * f(SCALE), s * f(SCALE), c, s], 1)
    c, s = rot(np.arange(N_CMP) * CMP_STRIDE + CMP_LEN - 1)
    mix[:, M_CROPE:M_CROPE + N_CMP] = c
    mix[:, M_CROPE + CP:M_CROPE + CP + N_CMP] = s
    end = np.arange(CP) * CMP_STRIDE + CMP_LEN - 1
    for t in range(TT):
        tok = t * P + np.arange(P)
        vis = (end[None, :] <= tok[:, None]) & (np.arange(CP) < N_CMP)[None, :]
        mix[:, M_CMASK + t * CP:M_CMASK + (t + 1) * CP] = np.where(vis, 0, NEG)
        mix[:, M_ANY + t] = vis.any(1)
    for h in range(HPG):
        for g in range(GROUPS):
            r = (g * HPG + h) * CP
            mix[r:r + CP, M_VSEL + h * P + g * HD:M_VSEL + h * P + (g + 1) * HD] = 1
    for g, w in enumerate(POOL_W):
        mix[:, M_CNT + g * T:M_CNT + (g + 1) * T] = f(1) / np.minimum(np.arange(T) + 1, w).astype(f)
    bf = np.zeros((P, 2 * P), f)
    bf[:, :P] = np.eye(P)
    bf[:, P:] = np.where(np.arange(P)[None, :] <= np.arange(P)[:, None], 0, NEG)
    return keep, mix, bf


def _layout(c, w_ada, b_ada, w_in, cmp_pe, cmp_w1, cmp_w2, w_pool, pool_scale, w_lift, w_o, ln_g, ln_b,
            peer_wq, peer_keys, peer_u, peer_v):
    stream = np.zeros((N_PRE + L * SLOTS + RING, P, D), np.float32)
    late = np.zeros((L, ADA_LATE, P, D), np.float32)
    att, kvw = HEADS * HD, 6 * GROUPS * HD
    order = []
    for h in range(HPG):
        for g in range(GROUPS):
            order += list(range((g * HPG + h) * HD, (g * HPG + h + 1) * HD))
    by_pairs = list(order)
    kv = lambda branch, kind: list(range(att + (branch * 2 + kind) * P, att + (branch * 2 + kind + 1) * P))
    order += kv(1, 0) + kv(2, 0) + kv(0, 0) + kv(0, 1) + kv(1, 1) + kv(2, 1)
    gates = list(range(att + kvw, att + kvw + 24))
    rest = list(range(att + kvw + 24, w_in.shape[2]))

    def tiles(w):
        k, n = w.shape
        return w.reshape(k // P, P, n // P, P).transpose(2, 1, 0, 3).reshape(n // P, P, (k // P) * P)

    pack = np.zeros((L, P, PACK), np.float32)
    for l in range(L):
        ada = w_ada[l].T.reshape(ADA, P, D)
        stream[l * ADA_PRE:(l + 1) * ADA_PRE], late[l] = ada[:ADA_PRE], ada[ADA_PRE:]
        s = stream[N_PRE + l * SLOTS:N_PRE + (l + 1) * SLOTS]
        s[0:10] = tiles(w_in[l][:, order])
        s[10].reshape(P, KT, P)[:, :, :24] = w_in[l][:, gates].reshape(KT, P, 24).transpose(1, 0, 2)
        s[11:S_PROJ] = tiles(w_in[l][:, rest])
        s[S_LIFT:S_OUT, :, :512] = tiles(w_lift[l, 0][by_pairs])
        s[S_LIFT:S_OUT, :, 512:] = tiles(w_lift[l, 1])
        s[S_OUT:S_QUERY] = w_o[l].reshape(KT, P, D)
        s[S_QUERY:S_KEYS] = tiles(peer_wq[l])
        s[S_KEYS] = peer_keys[l].transpose(1, 3, 0, 2).reshape(P, D)
        s[S_UP:S_DOWN] = peer_u[l].reshape(NK, P, KT, P).transpose(0, 3, 2, 1).reshape(NK, P, D)
        s[S_DOWN:] = peer_v[l].reshape(NK, P, D)
        p = pack[l]
        w1 = p[:, W_CMP1:W_CMP2].reshape(P, 2, CMP_LEN, P)
        w2 = p[:, W_CMP2:W_PE].reshape(P, 2, P)
        for g in range(GROUPS):
            r = slice(g * HD, (g + 1) * HD)
            w1[r, :, :, r] = cmp_w1[l].reshape(2, CMP_LEN, HD, HD).transpose(2, 0, 1, 3)
            w2[r, :, r] = cmp_w2[l].transpose(1, 0, 2)
            p[r, W_PE:W_POOL] = cmp_pe[l].transpose(2, 0, 1).reshape(HD, 2 * CMP_LEN)
        p[:, W_CMP1:W_CMP2] = w1.reshape(P, -1)
        p[:, W_CMP2:W_PE] = w2.reshape(P, -1)
        p[:, W_POOL:W_PSC] = w_pool[l].transpose(1, 0, 2).reshape(P, POOL_G * P)
        p[:, W_PSC:] = pool_scale[l].reshape(POOL_G, P).T
    ln_gb = np.stack([ln_g[:, 0], ln_b[:, 0], ln_g[:, 1], ln_b[:, 1]], 1).reshape(L, 4, 1, D)
    before = np.zeros((P, 2 * L, 2, KT), np.float32)
    before[:, 0, 0] = 1
    for n in range(2 * L - 1):
        before[:, n + 1, 0] = ln_g[n // 2, n % 2].reshape(KT, P).T
        before[:, n + 1, 1] = ln_b[n // 2, n % 2].reshape(KT, P).T
    return stream, late, before, np.ascontiguousarray(b_ada.reshape(L * ADA, P).T), pack, np.ascontiguousarray(ln_gb)


def kernel(x, c, w_ada, b_ada, w_in, cmp_pe, cmp_w1, cmp_w2, w_pool, pool_scale, w_lift, w_o,
           ln_g, ln_b, peer_wq, peer_keys, peer_u, peer_v):
    import concourse.bacc as bacc
    from concourse.bass_utils import run_bass_kernel_spmd

    weights = [np.asarray(a) for a in (c, w_ada, b_ada, w_in, cmp_pe, cmp_w1, cmp_w2, w_pool, pool_scale, w_lift,
                                       w_o, ln_g, ln_b, peer_wq, peer_keys, peer_u, peer_v)]
    stream, late, before, bias, pack, ln_gb = _layout(*weights)
    keep, mix, bf = _tables()
    arrays = {"in_stream": stream, "in_late": late, "in_before": before, "in_x": np.ascontiguousarray(x), "in_c": np.ascontiguousarray(c), "in_b_ada": bias,
              "in_pack": pack, "in_ln": ln_gb, "in_keep": keep, "in_mix": mix, "in_bf": bf}
    nc = bacc.Bacc("TRN2", target_bir_lowering=False, num_devices=1)
    aps = [nc.dram_tensor(n, a.shape, mybir.dt.from_np(a.dtype), kind="ExternalInput").ap() for n, a in arrays.items()]
    out = nc.dram_tensor("out_x", (1, T, D), F32, kind="ExternalOutput").ap()
    program(nc, *aps, out)
    r = run_bass_kernel_spmd(nc, [arrays], core_ids=[0])
    return r.results[0]["out_x"]
```
